# Optimizing a Trainium2 kernel written in Bass

```python
import jax
import jax.numpy as jnp
from jax import lax
import numpy as np

D_MODEL = 1024
BATCH = 1
SEQ = 512
DEPTH = 2

GRID_W = 64
CTX_LEN = 256
EPS = 1e-6

F_GROUPS = 4
F_DIM = 64
F_WIDTH = F_GROUPS * F_DIM

MLA_HEADS = 6
MLA_Q_LORA = 192
MLA_KV_LORA = 128
MLA_NOPE = 64
MLA_ROPE = 32
MLA_V = 64
MLA_QK = MLA_NOPE + MLA_ROPE
MLA_WIDTH = MLA_HEADS * MLA_V
MLA_IN = MLA_Q_LORA + MLA_KV_LORA + MLA_ROPE
ROPE_BASE = 10000.0
Q_BLOCK = 128

GLA_HEADS = 4
GLA_DK = 48
GLA_DV = 96
GLA_GATE_RANK = 16
GLA_GATE_NORM = 16.0
GLA_CHUNK = 64
GLA_WIDTH = GLA_HEADS * GLA_DV
GLA_QK_W = GLA_HEADS * GLA_DK
GLA_IN = 2 * GLA_QK_W + 2 * GLA_WIDTH + GLA_GATE_RANK

MIX_WIDTH = F_WIDTH + MLA_WIDTH + GLA_WIDTH
IN_COLS = F_WIDTH + MLA_IN + GLA_IN
D_FF = 2816
CONV_W = 3
N_MOD = 6

kernel_name = "hybrid_fourier_mla_gla_dit_block"

def rms_norm(x, w):
    xf = x.astype(jnp.float32)
    y = xf * lax.rsqrt(jnp.mean(xf * xf, axis=-1, keepdims=True) + EPS)
    return y.astype(x.dtype) * w

def modulate(h, shift, scale):
    return h * (1 + scale) + shift

def adaln(cond, w_mod, b_mod):
    m = jax.nn.silu(cond) @ w_mod + b_mod
    return jnp.split(m, N_MOD, axis=-1)

def to_heads(t, n_heads, d):
    B, L, _ = t.shape
    return t.reshape(B, L, n_heads, d).transpose(0, 2, 1, 3)

def from_heads(t):
    B, H, L, d = t.shape
    return t.transpose(0, 2, 1, 3).reshape(B, L, H * d)

def axial_angles(n_tokens):
    rows = n_tokens // GRID_W
    row = jnp.repeat(jnp.arange(rows, dtype=jnp.float32), GRID_W)
    col = jnp.tile(jnp.arange(GRID_W, dtype=jnp.float32), rows)
    axis_dims = MLA_ROPE // 2
    inv_freq = jnp.power(ROPE_BASE, -jnp.arange(0, axis_dims, 2, dtype=jnp.float32) / axis_dims)
    return row[:, None] * inv_freq, col[:, None] * inv_freq

def rotate_half_pairs(t, ang):
    t1, t2 = jnp.split(t, 2, axis=-1)
    cos = jnp.cos(ang).astype(t.dtype)
    sin = jnp.sin(ang).astype(t.dtype)
    return jnp.concatenate([t1 * cos - t2 * sin, t1 * sin + t2 * cos], axis=-1)

def rope_part(t, ang_r, ang_c):
    t_nope, t_rope = t[..., :MLA_NOPE], t[..., MLA_NOPE:]
    t_r, t_c = jnp.split(t_rope, 2, axis=-1)
    return jnp.concatenate([t_nope, rotate_half_pairs(t_r, ang_r), rotate_half_pairs(t_c, ang_c)], axis=-1)

def fourier_mix(f):
    B, L, _ = f.shape
    fg = f.astype(jnp.float32).reshape(B, L, F_GROUPS, F_DIM)
    y = jnp.fft.fft2(fg, axes=(1, 3), norm="ortho").real
    return y.reshape(B, L, F_WIDTH).astype(f.dtype)

def mla_q(p, q_lora_norm_w, w_uq, q_norm_w, ang_r, ang_c):
    B, L, _ = p.shape
    c_q = p[..., :MLA_Q_LORA]
    q = (rms_norm(c_q, q_lora_norm_w) @ w_uq).reshape(B, L, MLA_HEADS, MLA_QK)
    q = rms_norm(q, q_norm_w).transpose(0, 2, 1, 3)
    if ang_r is not None:
        q = rope_part(q, ang_r, ang_c)
    return q

def mla_kv(p, kv_lora_norm_w, w_ukv, k_norm_w, ang_r, ang_c):
    B, L, _ = p.shape
    c_kv = p[..., MLA_Q_LORA:MLA_Q_LORA + MLA_KV_LORA]
    k_pe = p[..., MLA_Q_LORA + MLA_KV_LORA:]
    kv = (rms_norm(c_kv, kv_lora_norm_w) @ w_ukv).reshape(B, L, MLA_HEADS, MLA_NOPE + MLA_V)
    k_nope, v = kv[..., :MLA_NOPE], kv[..., MLA_NOPE:]
    k = jnp.concatenate([k_nope, jnp.broadcast_to(k_pe[:, :, None, :], (B, L, MLA_HEADS, MLA_ROPE))], axis=-1)
    k = rms_norm(k, k_norm_w).transpose(0, 2, 1, 3)
    if ang_r is not None:
        k = rope_part(k, ang_r, ang_c)
    return k, v.transpose(0, 2, 1, 3)

def blocked_attention(q, k, v):
    B, H, L, dk = q.shape
    nb = L // Q_BLOCK
    scale = MLA_QK ** -0.5
    qb = q.reshape(B, H, nb, Q_BLOCK, dk).transpose(2, 0, 1, 3, 4)

    def one_block(q_blk):
        s = jnp.einsum("bhqd,bhkd->bhqk", q_blk, k).astype(jnp.float32) * scale
        pr = jax.nn.softmax(s, axis=-1).astype(v.dtype)
        return jnp.einsum("bhqk,bhkv->bhqv", pr, v)

    ob = lax.map(one_block, qb)
    return ob.transpose(1, 2, 0, 3, 4).reshape(B, H, L, v.shape[-1])

def gla_chunked(q, k, v, g, s0):
    B, H, T, dk = q.shape
    dv = v.shape[-1]
    n = T // GLA_CHUNK
    f32 = jnp.float32
    qc = q.astype(f32).reshape(B, H, n, GLA_CHUNK, dk)
    kc = k.astype(f32).reshape(B, H, n, GLA_CHUNK, dk)
    vc = v.astype(f32).reshape(B, H, n, GLA_CHUNK, dv)
    b = jnp.cumsum(g.astype(f32).reshape(B, H, n, GLA_CHUNK, dk), axis=3)
    b_last = b[:, :, :, -1:, :]
    q_in = qc * jnp.exp(b)
    k_in = kc * jnp.exp(-b)
    k_out = kc * jnp.exp(b_last - b)
    mask = jnp.tril(jnp.ones((GLA_CHUNK, GLA_CHUNK), dtype=bool))
    a = jnp.where(mask, jnp.einsum("bhncd,bhnsd->bhncs", q_in, k_in), 0.0)
    o_intra = jnp.einsum("bhncs,bhnsv->bhncv", a, vc)
    u = jnp.einsum("bhnsd,bhnsv->bhndv", k_out, vc)
    decay = jnp.exp(b_last[:, :, :, 0, :])

    def step(s, inp):
        dec, inc = inp
        return dec[..., None] * s + inc, s

    s_fin, s_prev = lax.scan(step, s0.astype(f32), (jnp.moveaxis(decay, 2, 0), jnp.moveaxis(u, 2, 0)))
    s_prev = jnp.moveaxis(s_prev, 0, 2)
    o_inter = jnp.einsum("bhncd,bhndv->bhncv", q_in, s_prev)
    return (o_intra + o_inter).reshape(B, H, T, dv), s_fin

def gla_parts(p):
    q, k, v, gk_lr, g = jnp.split(p, [GLA_QK_W, 2 * GLA_QK_W, 2 * GLA_QK_W + GLA_WIDTH,
                                      2 * GLA_QK_W + GLA_WIDTH + GLA_GATE_RANK], axis=-1)
    return (to_heads(q, GLA_HEADS, GLA_DK) * (GLA_DK ** -0.5), to_heads(k, GLA_HEADS, GLA_DK),
            to_heads(v, GLA_HEADS, GLA_DV), gk_lr, g)

def gla_log_decay(gk_lr, w_gk, b_gk):
    g = jax.nn.log_sigmoid((gk_lr @ w_gk + b_gk).astype(jnp.float32)) / GLA_GATE_NORM
    return to_heads(g, GLA_HEADS, GLA_DK)

def gla_direction(parts_x, parts_c, w_gk, b_gk, reverse):
    flip = (lambda t: jnp.flip(t, axis=2)) if reverse else (lambda t: t)
    qx, kx, vx, lx, _ = parts_x
    qc, kc, vc, lc, _ = parts_c
    B = qx.shape[0]
    s0 = jnp.zeros((B, GLA_HEADS, GLA_DK, GLA_DV), jnp.float32)
    o_c, s_c = gla_chunked(flip(qc), flip(kc), flip(vc), flip(gla_log_decay(lc, w_gk, b_gk)), s0)
    o_x, _ = gla_chunked(flip(qx), flip(kx), flip(vx), flip(gla_log_decay(lx, w_gk, b_gk)), s_c)
    return flip(o_x), flip(o_c)

def gla_output(o, g, norm_w):
    B, H, T, dv = o.shape
    o = rms_norm(o.transpose(0, 2, 1, 3).astype(g.dtype), norm_w).reshape(B, T, H * dv)
    return o * jax.nn.silu(g)

def token_mixer(h_x, h_c, ang_r, ang_c, w_in, mla_q_lora_norm_w, mla_w_uq, mla_kv_lora_norm_w,
                mla_w_ukv, mla_q_norm_w, mla_k_norm_w, gla_w_gk_fwd, gla_b_gk_fwd, gla_w_gk_bwd,
                gla_b_gk_bwd, gla_norm_w, w_out, need_ctx_out):
    p_x = h_x @ w_in
    p_c = h_c @ w_in
    f_x, m_x, g_x = jnp.split(p_x, [F_WIDTH, F_WIDTH + MLA_IN], axis=-1)
    f_c, m_c, g_c = jnp.split(p_c, [F_WIDTH, F_WIDTH + MLA_IN], axis=-1)
    k_c, v_c = mla_kv(m_c, mla_kv_lora_norm_w, mla_w_ukv, mla_k_norm_w, None, None)
    k_x, v_x = mla_kv(m_x, mla_kv_lora_norm_w, mla_w_ukv, mla_k_norm_w, ang_r, ang_c)
    q_x = mla_q(m_x, mla_q_lora_norm_w, mla_w_uq, mla_q_norm_w, ang_r, ang_c)
    a_x = blocked_attention(q_x, jnp.concatenate([k_c, k_x], axis=2), jnp.concatenate([v_c, v_x], axis=2))
    parts_x, parts_c = gla_parts(g_x), gla_parts(g_c)
    ox_f, oc_f = gla_direction(parts_x, parts_c, gla_w_gk_fwd, gla_b_gk_fwd, False)
    ox_b, oc_b = gla_direction(parts_x, parts_c, gla_w_gk_bwd, gla_b_gk_bwd, True)
    lin_x = gla_output(ox_f + ox_b, parts_x[4], gla_norm_w)
    y_x = jnp.concatenate([fourier_mix(f_x), from_heads(a_x), lin_x], axis=-1) @ w_out
    if not need_ctx_out:
        return y_x, None
    q_c = mla_q(m_c, mla_q_lora_norm_w, mla_w_uq, mla_q_norm_w, None, None)
    a_c = blocked_attention(q_c, k_c, v_c)
    lin_c = gla_output(oc_f + oc_b, parts_c[4], gla_norm_w)
    y_c = jnp.concatenate([fourier_mix(f_c), from_heads(a_c), lin_c], axis=-1) @ w_out
    return y_x, y_c

def conv_ffn(h, w_12, conv_w, conv_b, w_down):
    u = h @ w_12
    up = jnp.pad(u, ((0, 0), (1, 1), (0, 0)))
    u = up[:, :-2] * conv_w[0] + up[:, 1:-1] * conv_w[1] + up[:, 2:] * conv_w[2] + conv_b
    a, b = jnp.split(u, 2, axis=-1)
    return (jax.nn.silu(a) * b) @ w_down

def setup_inputs(seed: int = 0) -> dict:
    key = jax.random.key(seed)
    keys = iter(jax.random.split(key, 32))

    def nrm(shape, scale):
        return jax.random.normal(next(keys), shape, jnp.float32) * scale

    def gain(shape):
        return 1.0 + 0.02 * jax.random.normal(next(keys), shape, jnp.float32)

    D = D_MODEL
    return {
        "x": nrm((BATCH, SEQ, D), 1.0),
        "c": nrm((BATCH, D), 1.0),
        "ctx": nrm((BATCH, CTX_LEN, D), 1.0),
        "c_ctx": nrm((D,), 1.0),
        "mod_w": nrm((DEPTH, D, N_MOD * D), D ** -0.5),
        "mod_b": nrm((DEPTH, N_MOD * D), 0.02),
        "norm1_w": gain((DEPTH, D)),
        "norm2_w": gain((DEPTH, D)),
        "w_in": nrm((DEPTH, D, IN_COLS), D ** -0.5),
        "mla_q_lora_norm_w": gain((DEPTH, MLA_Q_LORA)),
        "mla_w_uq": nrm((DEPTH, MLA_Q_LORA, MLA_HEADS * MLA_QK), MLA_Q_LORA ** -0.5),
        "mla_kv_lora_norm_w": gain((DEPTH, MLA_KV_LORA)),
        "mla_w_ukv": nrm((DEPTH, MLA_KV_LORA, MLA_HEADS * (MLA_NOPE + MLA_V)), MLA_KV_LORA ** -0.5),
        "mla_q_norm_w": gain((DEPTH, MLA_QK)),
        "mla_k_norm_w": gain((DEPTH, MLA_QK)),
        "gla_w_gk_fwd": nrm((DEPTH, GLA_GATE_RANK, GLA_QK_W), GLA_GATE_RANK ** -0.5),
        "gla_b_gk_fwd": nrm((DEPTH, GLA_QK_W), 0.02),
        "gla_w_gk_bwd": nrm((DEPTH, GLA_GATE_RANK, GLA_QK_W), GLA_GATE_RANK ** -0.5),
        "gla_b_gk_bwd": nrm((DEPTH, GLA_QK_W), 0.02),
        "gla_norm_w": gain((DEPTH, GLA_DV)),
        "w_out": nrm((DEPTH, MIX_WIDTH, D), MIX_WIDTH ** -0.5),
        "ffn_w_12": nrm((DEPTH, D, 2 * D_FF), D ** -0.5),
        "ffn_conv_w": nrm((DEPTH, CONV_W, 2 * D_FF), CONV_W ** -0.5),
        "ffn_conv_b": nrm((DEPTH, 2 * D_FF), 0.02),
        "ffn_w_down": nrm((DEPTH, D_FF, D), D_FF ** -0.5),
    }

def reference(x, c, ctx, c_ctx, mod_w, mod_b, norm1_w, norm2_w, w_in, mla_q_lora_norm_w, mla_w_uq,
              mla_kv_lora_norm_w, mla_w_ukv, mla_q_norm_w, mla_k_norm_w, gla_w_gk_fwd, gla_b_gk_fwd,
              gla_w_gk_bwd, gla_b_gk_bwd, gla_norm_w, w_out, ffn_w_12, ffn_conv_w, ffn_conv_b, ffn_w_down):
    ang_r, ang_c = axial_angles(x.shape[1])
    xc = ctx
    for l in range(DEPTH):
        last = l == DEPTH - 1
        sh1, sc1, g1, sh2, sc2, g2 = [m[:, None, :] for m in adaln(c, mod_w[l], mod_b[l])]
        csh1, csc1, cg1, csh2, csc2, cg2 = adaln(c_ctx, mod_w[l], mod_b[l])
        h_x = modulate(rms_norm(x, norm1_w[l]), sh1, sc1)
        h_c = modulate(rms_norm(xc, norm1_w[l]), csh1, csc1)
        y_x, y_c = token_mixer(h_x, h_c, ang_r, ang_c, w_in[l], mla_q_lora_norm_w[l], mla_w_uq[l],
                               mla_kv_lora_norm_w[l], mla_w_ukv[l], mla_q_norm_w[l], mla_k_norm_w[l],
                               gla_w_gk_fwd[l], gla_b_gk_fwd[l], gla_w_gk_bwd[l], gla_b_gk_bwd[l],
                               gla_norm_w[l], w_out[l], not last)
        x = x + g1 * y_x
        h_x = modulate(rms_norm(x, norm2_w[l]), sh2, sc2)
        x = x + g2 * conv_ffn(h_x, ffn_w_12[l], ffn_conv_w[l], ffn_conv_b[l], ffn_w_down[l])
        if not last:
            xc = xc + cg1 * y_c
            h_c = modulate(rms_norm(xc, norm2_w[l]), csh2, csc2)
            xc = xc + cg2 * conv_ffn(h_c, ffn_w_12[l], ffn_conv_w[l], ffn_conv_b[l], ffn_w_down[l])
    return x


_drawn_inputs = setup_inputs


def setup_inputs(seed=0):
    import zlib

    import numpy as np

    out = dict(_drawn_inputs(seed))
    spreads = {}
    factors = {'norm1_w': 3.37,
     'norm2_w': 2.924,
     'mla_q_lora_norm_w': 8.0,
     'mla_kv_lora_norm_w': 8.0,
     'mla_q_norm_w': 8.0,
     'mla_k_norm_w': 8.0,
     'gla_b_gk_fwd': 8.0,
     'gla_b_gk_bwd': 8.0,
     'gla_norm_w': 6.743,
     'ffn_conv_b': 3.486}
    for name, (base, spread) in spreads.items():
        noise = np.random.default_rng([zlib.crc32(name.encode()), seed]).standard_normal(out[name].shape)
        drawn = base * np.exp(spread * noise) if base else spread * noise
        out[name] = jnp.asarray(drawn.astype(out[name].dtype))
    for name, factor in factors.items():
        out[name] = (out[name] * factor).astype(out[name].dtype)
    return out
```

```python
from contextlib import ExitStack

import concourse.bass as bass
import numpy as np
from concourse import mybir

F32 = mybir.dt.float32
F32R = mybir.dt.float32r
I32 = mybir.dt.int32
ALU = mybir.AluOpType
ACT = mybir.ActivationFunctionType
AX_X = mybir.AxisListType.X

DEPTH, D, NX, NC = 2, 1024, 512, 256
NT = NX + NC
P = 128
KD = D // P
EPS = 1e-6
F_DIM, F_WIDTH = 64, 256
HEADS, Q_LORA, KV_LORA, NOPE, ROPE, VDIM = 6, 192, 128, 64, 32, 64
QK = NOPE + ROPE
QH = Q_LORA // 2
GH, DK, DV, RANK, CHUNK = 4, 48, 96, 16, 64
GRID_W, ROPE_BASE, GATE_NORM = 64, 10000.0, 16.0
D_FF = 2816
NPAIR = D_FF // P
SCALE = QK ** -0.5
NCH = NT // CHUNK

RING = 4
SPLIT = 2
PARTS = (8, 8, 6)
KOUT = 9
SLOT = KOUT * P
MOD_A, MOD_B = 16, 32
NMOD = MOD_A + MOD_B
INP_UNITS = 16
(U_CQ0, U_CQ1, U_CKV, U_K01, U_K23, U_V0, U_V1, U_V2,
 U_F0, U_F1, U_Q01, U_Q23, U_G0, U_G1, U_G2, U_G3) = range(INP_UNITS)
NSPLIT = INP_UNITS + KD + 2 * NPAIR + KD * len(PARTS)


def four_tiles(l):
    return 8 if l < DEPTH - 1 else 4


def raw_base(l):
    return sum(NMOD + four_tiles(m) + NSPLIT for m in range(l))


def raw_to_users(g):
    l = 0
    while g >= raw_base(l + 1):
        l += 1
    i = g - raw_base(l)
    whole = sum(NMOD + four_tiles(m) for m in range(l))
    if i < NMOD:
        return "whole", whole + i
    i -= NMOD
    if i < INP_UNITS:
        return "split", l * NSPLIT + i
    i -= INP_UNITS
    if i < four_tiles(l):
        return "whole", whole + NMOD + i
    return "split", l * NSPLIT + INP_UNITS + i - four_tiles(l)


V_MODB, V_N1, V_N2, V_QL, V_KVL, V_QW, V_KW, V_GN, V_CONV = 0, 48, 56, 64, 66, 67, 68, 69, 70
NV = V_CONV + NPAIR * 8


def build_trunk(nc, x_t, c_t, vec, w_mod, w_inp, w_four_x, w_four_c, w_outp, w_up, w_dn0, w_dn1, w_dn2,
                w_uq, w_ukv, w_gk, k_ident, k_tri, k_mask, k_rope, k_rot, k_dft, out):
    w_dn = (w_dn0, w_dn1, w_dn2)
    place = [(nc.sbuf_base + 31) // 32 * 32]

    def at(name, shape, offset, dt=F32):
        return nc.alloc_sbuf_tensor_at(name, shape, dt, offset=offset)

    def keep(name, shape, dt=F32):
        n = int(np.prod(shape[1:])) * 4
        t = at(name, shape, place[0], dt)
        place[0] += (n + 31) // 32 * 32
        return t

    xt = keep("xt", [P, KD, NT])
    raw = [keep(f"raw{s}", [P, SLOT]) for s in range(RING)]
    whi = [keep(f"whi{s}", [P, SLOT], F32R) for s in range(SPLIT)]
    wlo = [keep(f"wlo{s}", [P, SLOT], F32R) for s in range(SPLIT)]
    ident = keep("ident", [P, P])
    ones = keep("ones", [P, P])
    tri = keep("tri", [P, 2, P])
    amask = keep("amask", [P, 2, P], I32)
    rope = keep("rope", [P, 2, NX])
    rot = keep("rot", [P, ROPE])
    dftf = keep("dftf", [P, 2 * P])
    eps = keep("eps", [P, 1])
    craw = keep("craw", [P, KD, 2])
    csil = keep("csil", [P, KD, 2])
    modv = keep("modv", [P, 6 * KD, 2])
    mscale = keep("mscale", [P, 2, KD, 2])
    par = keep("par", [P, DEPTH, NV])
    mx = keep("mx", [P, 2])
    nmx = keep("nmx", [P, 2])
    rsum = keep("rsum", [P, 2])
    rinv = keep("rinv", [P, 2])
    blast = keep("blast", [P, NCH])
    decay = keep("decay", [P, NCH])
    uq = keep("uq", [QH, 2, HEADS * QK])
    ukv = keep("ukv", [P, HEADS * (NOPE + VDIM)])
    wgk = keep("wgk", [RANK + 1, GH * P])

    arena = place[0]

    def ar(name, shape, kib, dt=F32):
        return at(name, shape, arena + int(kib * 1024), dt)

    qp = ar("qp", [P, 2, NT], 0)
    kp = ar("kp", [P, 2, NT], 6)
    gs = ar("gs", [P, GH, NT], 12)
    vtok = ar("vtok", [P, 6, GH * DV], 24)
    lr = ar("lr", [32, NT], 33)
    ft = ar("ft", [P, 2, NT], 36)
    cq = ar("cq", [QH, 2, NT], 42)
    ckv = ar("ckv", [P, NT], 48)
    kpe = ar("kpe", [P, NT], 51)
    hhi = ar("hhi", [P, KD, NT], 54, F32R)
    hlo = ar("hlo", [P, KD, NT], 78, F32R)
    vt = ar("vt", [P, 3, NT], 102)
    rstd = ar("rstd", [P, NT], 102)
    sq = [ar(f"sq{i}", [P, NT], 105 + 3 * i) for i in range(2)]
    xn = [ar(f"xn{i}", [P, NT], 111 + 3 * i) for i in range(2)]
    hf = [ar(f"hf{i}", [P, NT], 117 + 3 * i) for i in range(2)]
    mixfa = ar("mixfa", [P, 5, NT], 54)
    gdft = ar("gdft", [P, 6, 4 * P], 69)
    qh = [ar(f"qh{i}", [QK, NT], 69 + 3 * i) for i in range(2)]
    kh = [ar(f"kh{i}", [QK, NT], 75 + 3 * i) for i in range(2)]
    vall = ar("vall", [P, 6, HEADS * VDIM], 81)
    pr = [ar(f"pr{i}", [P, NT], 90 + 3 * i) for i in range(2)]
    ptx = ar("ptx", [P, 6, NX], 96)
    rsq = ar("rsq", [P, NT], 108)
    rsk = ar("rsk", [P, NT], 111)
    ksq = ar("ksq", [P, NT], 114)
    rtmp = ar("rtmp", [P, NX], 117)
    ptc = ar("ptc", [P, 2, NC], 120)
    qsq = [ar(f"qsq{i}", [P, NT], 36 + 3 * i) for i in range(2)]
    gtok = ar("gtok", [P, 6, GH * P], 36)
    e_pos = ar("e_pos", [P, NT], 48)
    e_neg = ar("e_neg", [P, NT], 51)
    e_out = ar("e_out", [P, NT], 69)
    qr = ar("qr", [P, NT], 72)
    kr = ar("kr", [P, NT], 75)
    kin = ar("kin", [P, NT], 78)
    ktok = ar("ktok", [P, 6, P], 81)
    st = ar("st", [P, NCH, DV], 84)
    am = [ar(f"am{i}", [P, NT], 89 + 3 * i) for i in range(2)]
    osq = ar("osq", [P, NT], 95)
    ors = ar("ors", [P, NT], 98)
    ga = ar("ga", [P, 2 * NX], 101)
    ot = ar("ot", [P, NT], 105)
    mhi = ar("mhi", [P, KOUT, NT], 69, F32R)
    mlo = ar("mlo", [P, KOUT, NT], 24, F32R)
    fhi = ar("fhi", [P, max(PARTS), NT], 0, F32R)
    flo = ar("flo", [P, max(PARTS), NT], 24, F32R)
    ca = [ar(f"ca{i}", [P, NT], 102 + 3 * i) for i in range(2)]
    cb = [ar(f"cb{i}", [P, NT], 108 + 3 * i) for i in range(2)]
    cf = [ar(f"cf{i}", [P, NT], 114 + 3 * i) for i in range(2)]

    def width(l):
        return NT if l < DEPTH - 1 else NX

    def chunks(n):
        return [(0, NX), (NX, NT)][: 1 if n == NX else 2]

    def streams(n):
        return [(0, NX, 0), (NX, NT, 1)][: 1 if n == NX else 2]

    def s_base(l):
        return l * NSPLIT

    def w_base(l):
        return sum(NMOD + four_tiles(m) for m in range(l))

    S_OUT = INP_UNITS

    def s_up(p):
        return INP_UNITS + KD + sum(2 * PARTS[q] + KD for q in range(p))

    def pair_base(l, p):
        return l * NPAIR + sum(PARTS[:p])

    def attn_units(l):
        return [("x", i * P) for i in range(NX // P)] + ([("c", NX + i * P) for i in range(NC // P)] if l < DEPTH - 1 else [])

    def u_base(l, h):
        return sum(HEADS * len(attn_units(m)) for m in range(l)) + h * len(attn_units(l))

    def u_col(c):
        return (4 + 2 * (c % 2) + c // 2 // 3) * 512 + (c // 2 % 3) * DV

    def o_base(l, h):
        per = [2 if m < DEPTH - 1 else 1 for m in range(DEPTH)]
        return sum(HEADS * per[m] for m in range(l)) + h * per[l]

    with ExitStack() as ctx:
        ps = ctx.enter_context(nc.psum_tensor("ps", [P, 8 * 512], F32))

        def acc(s, a=0, b=NT, rows=(0, P)):
            return ps[rows[0]:rows[1], s * 1024 + a:s * 1024 + b]

        def bank(k, a=0, b=512, rows=(0, P)):
            return ps[rows[0]:rows[1], k * 512 + a:k * 512 + b]

        def sem(name):
            return ctx.enter_context(nc.semaphore(name))

        const_in, table_in, x_in, small_in, stored = (sem(n) for n in ("const_in", "table_in", "x_in", "small_in", "stored"))
        raw_in = [sem(f"raw_in{s}") for s in range(RING)]
        whole_used = sem("whole_used")
        hi_ready, lo_ready = sem("hi_ready"), sem("lo_ready")
        unit_done = sem("unit_done")
        pe_bar, act_bar, dve_bar = sem("pe_bar"), sem("act_bar"), sem("dve_bar")
        act_step, dve_step = sem("act_step"), sem("dve_step")
        ready0, csil_ready = sem("ready0"), sem("csil_ready")
        mod_ready = sem("mod_ready")
        sq_ready, sq_used, ssq_done = sem("sq_ready"), sem("sq_used"), sem("ssq_done")
        rstd_ready, xn_ready, xn_used = sem("rstd_ready"), sem("xn_ready"), sem("xn_used")
        hh_ready, h_ready = sem("hh_ready"), sem("h_ready")
        evac_a, evac_d = sem("evac_a"), sem("evac_d")
        vtr_done, vtr_a, vtr_d = sem("vtr_done"), sem("vtr_a"), sem("vtr_d")
        gd_done, gd_a, gd_d, four_done = sem("gd_done"), sem("gd_a"), sem("gd_d"), sem("four_done")
        lat_sq, lat_ssq, lat_rs, lat_n = sem("lat_sq"), sem("lat_ssq"), sem("lat_rs"), sem("lat_n")
        kpw_ready, kpe_rot, va_done, va_a, va_d = sem("kpw_ready"), sem("kpe_rot"), sem("va_done"), sem("va_a"), sem("va_d")
        qk_done, qksq_ready, qkssq_done, qkrs_ready = sem("qk_done"), sem("qksq_ready"), sem("qkssq_done"), sem("qkrs_ready")
        qn_ready, qrot_done, qk_ready = sem("qn_ready"), sem("qrot_done"), sem("qk_ready")
        s_done, mx_ready, p_exp, p_ready = sem("s_done"), sem("mx_ready"), sem("p_exp"), sem("p_ready")
        t_done, pt_a, pt_d, pv_done, o_out = sem("t_done"), sem("pt_a"), sem("pt_d"), sem("pv_done"), sem("o_out")
        z_done, ls_ready, g_ready = sem("z_done"), sem("ls_ready"), sem("g_ready")
        b_done, e_ready, eo_raw, eo_ready, gq_ready, gk_ready = (sem(n) for n in ("b_done", "e_ready", "eo_raw", "eo_ready", "gq_ready", "gk_ready"))
        kt_done, ktok_ready, ud_done, st_ready, a_done, am_ready = (sem(n) for n in ("kt_done", "ktok_ready", "ud_done", "st_ready", "a_done", "am_ready"))
        go_done, osq_ready, ossq_done, ors_ready, lin_ready = (sem(n) for n in ("go_done", "osq_ready", "ossq_done", "ors_ready", "lin_ready"))
        mhi_ready, mlo_ready, x_upd = sem("mhi_ready"), sem("mlo_ready"), sem("x_upd")
        center_ready, gate_ready, side_ready, silu_ready = (sem(n) for n in ("center_ready", "gate_ready", "side_ready", "silu_ready"))
        fh_ready, hidh_ready, hid_ready, kpe_sq = (sem(n) for n in ("fh_ready", "hidh_ready", "hid_ready", "kpe_sq"))

        NCONST, NTABLE = 3, 5

        class Chain:

            def __init__(self, eng, own):
                self.eng, self.own, self.n, self.off = eng, own, 0, None

            def step(self, ins):
                ins.then_inc(self.own, 1)
                self.n += 1

            def wait(self, back=0):
                n = self.n - back
                self.eng.wait_ge(self.own, n if self.off is None else self.off + n)

        block = ctx.enter_context(nc.Block())

        @block.sync
        def _(sp):
            sp.dma_start(craw[:].rearrange("p a b -> p (a b)"), c_t).then_inc(const_in, 16)
            sp.dma_start(par[:].rearrange("p a b -> p (a b)"), vec).then_inc(const_in, 16)
            sp.dma_start(ident[:], k_ident).then_inc(const_in, 16)

            def wait_free(g):
                kind, n = raw_to_users(g)
                sp.wait_ge(whole_used if kind == "whole" else lo_ready, n + 1)

            def load(g, src, w):
                if g >= RING:
                    wait_free(g - RING)
                sp.dma_start(raw[g % RING][:, 0:w], src).then_inc(raw_in[g % RING], 16)

            def load_run(g0, n, src, w):
                for i in range(min(RING, n)):
                    load(g0 + i, src(i), w)
                if n > RING:
                    kind, m = raw_to_users(g0)
                    used = whole_used if kind == "whole" else lo_ready
                    with sp.Fori(1, n // RING) as it:
                        for s in range(RING):
                            sp.wait_ge(used, it * RING + (m + s + 1 - RING))
                            sp.dma_start(raw[(g0 + s) % RING][:, 0:w], src(it * RING + s)).then_inc(raw_in[(g0 + s) % RING], 16)

            for l in range(DEPTH):
                g = raw_base(l)
                load_run(g, NMOD, lambda i: w_mod[l, i], KD * P)
                g += NMOD
                load_run(g, INP_UNITS, lambda i: w_inp[l, i], KD * P)
                g += INP_UNITS
                load_run(g, 4, lambda i: w_four_x[i], 4 * 2 * P)
                g += 4
                if l < DEPTH - 1:
                    load_run(g, 4, lambda i: w_four_c[i], 2 * 2 * CHUNK)
                    g += 4
                load_run(g, KD, lambda i: w_outp[l, i], KOUT * P)
                g += KD
                at_pair = 0
                for p, n in enumerate(PARTS):
                    first = 2 * at_pair
                    load_run(g, 2 * n, lambda i: w_up[l, i + first], KD * P)
                    g += 2 * n
                    load_run(g, KD, lambda i: w_dn[p][l, i], n * P)
                    g += KD
                    at_pair += n
            sp.wait_ge(x_upd, DEPTH * KD * (1 + len(PARTS)))
            sp.dma_start(out, xt[:, :, 0:NX]).then_inc(stored, 16)
            sp.wait_ge(stored, 16)

        @block.gpsimd
        def _(pool):
            for k in range(KD):
                pool.dma_start(xt[:, k, :], x_t[:, k, :]).then_inc(x_in, 16)
            pool.dma_start(tri[:].rearrange("p a b -> p (a b)"), k_tri).then_inc(table_in, 16)
            pool.dma_start(amask[:].rearrange("p a b -> p (a b)"), k_mask).then_inc(table_in, 16)
            pool.dma_start(rope[NOPE:QK, :, :].rearrange("p a b -> p (a b)"), k_rope).then_inc(table_in, 16)
            pool.dma_start(rot[NOPE:QK, :], k_rot).then_inc(table_in, 16)
            pool.dma_start(dftf[:], k_dft).then_inc(table_in, 16)
            for l in range(DEPTH):
                if l:
                    pool.wait_ge(pe_bar, 4 * l)
                pool.dma_start(uq[:].rearrange("p a b -> p (a b)"), w_uq[l]).then_inc(small_in, 16)
                pool.dma_start(ukv[:], w_ukv[l]).then_inc(small_in, 16)
                pool.dma_start(wgk[:], w_gk[l]).then_inc(small_in, 16)

        @block.tensor
        def _(pe):
            mm = nc.tensor.matmul
            bar = [0]

            def barrier():
                bar[0] += 1
                nc.tensor.drain().then_inc(pe_bar, 1)
                pe.wait_ge(act_bar, bar[0])
                pe.wait_ge(dve_bar, bar[0])

            def modulation(l, first, n, col0):
                g0, w0 = raw_base(l) + first, w_base(l) + first
                with pe.Fori(0, n // RING) as it:
                    for s in range(RING):
                        pe.wait_ge(raw_in[(g0 + s) % RING], it * 16 + 16 * ((g0 + s) // RING + 1))
                        for k in range(KD):
                            last = mm(ps[:, bass.ds(it * (2 * RING) + (col0 + 2 * s), 2)],
                                      raw[(g0 + s) % RING][:, k * P:(k + 1) * P], csil[:, k, :],
                                      start=(k == 0), stop=(k == KD - 1))
                        last.then_inc(whole_used, 1)

            def sum_squares(n_norm, n):
                for k in range(KD):
                    pe.wait_ge(sq_ready, n_norm * KD + k + 1)
                    for a, b in chunks(n):
                        last = mm(acc(0, a, b), ones[:], sq[k % 2][:, a:b], start=(k == 0), stop=(k == KD - 1))
                    last.then_inc(ssq_done, 1)

            def product(s, slot, hi, lo, rows, n):
                last = len(rows) - 1
                for k, r in enumerate(rows):
                    wh, wl = whi[slot][0:r, k * P:(k + 1) * P], wlo[slot][0:r, k * P:(k + 1) * P]
                    for w, y in ((wh, hi), (wh, lo), (wl, hi)):
                        for a, b in chunks(n):
                            ins = mm(acc(s, a, b), w, y[0:r, k, a:b], start=(k == 0 and w is wh and y is hi),
                                     stop=(k == last and w is wl))
                ins.then_inc(unit_done, 1)

            pe.wait_ge(const_in, 16 * NCONST)
            pe.wait_ge(table_in, 16 * NTABLE)
            pe.wait_ge(ready0, 1)
            pe.wait_ge(csil_ready, 1)
            for l in range(DEPTH):
                n = width(l)
                if l:
                    pe.wait_ge(x_upd, l * KD * 4)
                modulation(l, 0, MOD_A, 6 * 512)
                sum_squares(2 * l, NT)
                modulation(l, MOD_A, MOD_B, 7 * 512)

                pe.wait_ge(h_ready, (2 * l + 1) * KD)
                for u in range(INP_UNITS):
                    pe.wait_ge(lo_ready, s_base(l) + u + 1)
                    if u == 3:
                        pe.wait_ge(mod_ready, 2 * l + 2)
                    if u >= 4 and u % 2 == 0:
                        pe.wait_ge(evac_a, l * 10 + (u - 4) // 2 + 1)
                    elif u >= 4:
                        pe.wait_ge(evac_d, l * 6 + (u - 5) // 2 + 1)
                    product(u % 4, u % 2, hhi, hlo, [P] * KD, NT if u < U_F0 or l < DEPTH - 1 else NX)
                barrier()

                for tt in range(6):
                    for j in range(3):
                        last = nc.tensor.transpose(bank(tt, j * P, (j + 1) * P), vt[:, j, tt * P:(tt + 1) * P], ident[:])
                    last.then_inc(vtr_done, 1)
                for tt in range(n // P):
                    if tt >= 2:
                        pe.wait_ge(gd_a if tt % 2 else gd_d, 3 * l + tt // 2)
                    for f in range(2):
                        last = mm(bank(6 + tt % 2, f * 2 * P, (f + 1) * 2 * P), ft[:, f, tt * P:(tt + 1) * P], dftf[:], start=True, stop=True)
                    last.then_inc(gd_done, 1)
                pe.wait_ge(vtr_d, 3 * l + 3)
                pe.wait_ge(vtr_a, 3 * l + 3)
                pe.wait_ge(gd_a, 3 * l + n // (2 * P))
                pe.wait_ge(gd_d, 3 * l + n // (2 * P))
                g0 = raw_base(l) + NMOD + INP_UNITS
                for blk in range(four_tiles(l)):
                    g = g0 + blk
                    pe.wait_ge(raw_in[g % RING], 16 * (g // RING + 1))
                    kt, w, first = (4, P, 0) if blk < 4 else (2, CHUNK, 4)
                    for f in range(2):
                        o = bank(f, blk * P, (blk + 1) * P) if blk < 4 else bank(2, f * NC + (blk - 4) * CHUNK, f * NC + (blk - 3) * CHUNK)
                        for k in range(kt):
                            for cs in range(2):
                                last = mm(o, gdft[:, first + k, f * 2 * P + cs * P:f * 2 * P + (cs + 1) * P],
                                          raw[g % RING][:, k * 2 * w + cs * w:k * 2 * w + (cs + 1) * w],
                                          start=(k == 0 and cs == 0), stop=(k == kt - 1 and cs == 1))
                    last.then_inc(whole_used, 1)
                barrier()

                pe.wait_ge(small_in, (l + 1) * 48)
                pe.wait_ge(lat_sq, 3 * l + 2)
                for a, b in chunks(NT):
                    mm(acc(0, a, b, (0, QH)), ones[0:QH, 0:QH], qsq[0][0:QH, a:b], start=True, stop=False)
                    last = mm(acc(0, a, b, (0, QH)), ones[0:QH, 0:QH], qsq[1][0:QH, a:b], start=False, stop=True)
                last.then_inc(lat_ssq, 1)
                pe.wait_ge(lat_sq, 3 * l + 3)
                for a, b in chunks(NT):
                    last = mm(acc(1, a, b), ones[:], ksq[:, a:b], start=True, stop=True)
                last.then_inc(lat_ssq, 1)
                pe.wait_ge(kpw_ready, l + 1)
                mm(acc(2, 0, NX, (NOPE, QK)), rot[NOPE:QK, :], kpe[NOPE:QK, 0:NX], start=True, stop=True).then_inc(kpe_rot, 1)
                pe.wait_ge(lat_n, 2 * l + 2)
                for tt in range(6):
                    if tt >= 2:
                        pe.wait_ge(va_a if tt % 2 else va_d, 3 * l + tt // 2)
                    mm(bank(6 + tt % 2, 0, HEADS * VDIM), ckv[:, tt * P:(tt + 1) * P],
                       ukv[:, HEADS * NOPE:HEADS * (NOPE + VDIM)], start=True, stop=True).then_inc(va_done, 1)
                pe.wait_ge(va_a, 3 * l + 3)
                pe.wait_ge(va_d, 3 * l + 3)

                for h in range(HEADS):
                    hh = l * HEADS + h
                    b2 = h % 2
                    if h:
                        pe.wait_ge(o_out, o_base(l, h))
                    for a, b in chunks(n):
                        for k in range(2):
                            last = mm(acc(0, a, b, (0, QK)), uq[:, k, h * QK:(h + 1) * QK], cq[:, k, a:b], start=(k == 0), stop=(k == 1))
                    last.then_inc(qk_done, 1)
                    for a, b in chunks(NT):
                        last = mm(acc(1, a, b, (0, NOPE)), ukv[:, h * NOPE:(h + 1) * NOPE], ckv[:, a:b], start=True, stop=True)
                    last.then_inc(qk_done, 1)
                    pe.wait_ge(qksq_ready, 2 * hh + 1)
                    if h:
                        pe.wait_ge(pt_a, u_base(l, h))
                        pe.wait_ge(pt_d, (l * HEADS + h) * 4)
                    for a, b in chunks(n):
                        last = mm(acc(2, a, b, (0, QK)), ones[0:QK, 0:QK], qsq[0][0:QK, a:b], start=True, stop=True)
                    last.then_inc(qkssq_done, 1)
                    pe.wait_ge(qksq_ready, 2 * hh + 2)
                    for a, b in chunks(NT):
                        last = mm(acc(3, a, b, (0, QK)), ones[0:QK, 0:QK], ksq[0:QK, a:b], start=True, stop=True)
                    last.then_inc(qkssq_done, 1)
                    pe.wait_ge(qn_ready, hh + 1)
                    mm(acc(2, 0, NX, (NOPE, QK)), rot[NOPE:QK, :], qh[b2][NOPE:QK, 0:NX], start=True, stop=True).then_inc(qrot_done, 1)
                    pe.wait_ge(qk_ready, hh + 1)

                    ub, units = u_base(l, h), attn_units(l)

                    def scores(j):
                        kind, q0 = units[j]
                        slot = (j if kind == "x" else j + 1) % 2
                        if 2 <= j < 5:
                            pe.wait_ge(p_exp, ub + (j - 1 if j < 4 else 4))
                        if j == 5:
                            pe.wait_ge(o_out, o_base(l, h) + 1)
                        for a, b in ([(0, NX), (NX, NT)] if kind == "x" else [(NX, NT)]):
                            last = mm(acc(slot, a, b), qh[b2][:, q0:q0 + P], kh[b2][:, a:b], start=True, stop=True)
                        last.then_inc(s_done, 1)

                    def turn(j):
                        kind, _ = units[j]
                        pe.wait_ge(p_ready, ub + j + 1)
                        if j >= 2:
                            pe.wait_ge(pt_a, ub + j - 1)
                            pe.wait_ge(pt_d, hh * 4 + j - 1)
                        for kt in (range(6) if kind == "x" else range(2)):
                            src = kt * P if kind == "x" else NX + kt * P
                            last = nc.tensor.transpose(acc(2 + j % 2, kt * P, (kt + 1) * P), pr[j % 2][:, src:src + P], ident[:])
                        last.then_inc(t_done, 1)

                    scores(0)
                    scores(1)
                    for j in range(4):
                        turn(j)
                        if j + 2 < 4:
                            scores(j + 2)
                    pe.wait_ge(pt_a, ub + 4)
                    pe.wait_ge(pt_d, hh * 4 + 4)
                    for kt in range(6):
                        last = mm(acc(0, 0, NX, (0, VDIM)), vall[:, kt, h * VDIM:(h + 1) * VDIM], ptx[:, kt, :], start=(kt == 0), stop=(kt == 5))
                    last.then_inc(pv_done, 1)
                    if l < DEPTH - 1:
                        scores(4)
                        scores(5)
                        turn(4)
                        turn(5)
                        pe.wait_ge(pt_a, ub + 6)
                        pe.wait_ge(p_exp, ub + 5)
                        for kt in range(2):
                            last = mm(acc(1, 0, NC, (0, VDIM)), vall[:, 4 + kt, h * VDIM:(h + 1) * VDIM], ptc[:, kt, :], start=(kt == 0), stop=(kt == 1))
                        last.then_inc(pv_done, 1)
                barrier()

                for tt in range(6):
                    mm(bank(tt), lr[0:RANK + 1, tt * P:(tt + 1) * P], wgk[:], start=True, stop=True).then_inc(z_done, 1)
                pe.wait_ge(g_ready, 3 * (l + 1))
                for h in range(GH):
                    hh = l * GH + h
                    if h:
                        pe.wait_ge(lin_ready, hh)
                    for tt in range(6):
                        for d in range(2):
                            last = mm(acc(0, tt * P, (tt + 1) * P, (64 * d, 64 * d + 64)), gtok[:, tt, h * P + 64 * d:h * P + 64 * d + 64],
                                      tri[:, d, :], start=True, stop=True)
                    last.then_inc(b_done, 1)
                    pe.wait_ge(gk_ready, hh + 1)
                    for tt in range(6):
                        last = nc.tensor.transpose(acc(1, tt * P, (tt + 1) * P), kr[:, tt * P:(tt + 1) * P], ident[:])
                    last.then_inc(kt_done, 1)
                    pe.wait_ge(gq_ready, hh + 1)
                    for d in range(2):
                        if d:
                            pe.wait_ge(ktok_ready, hh + 1)
                        for tt in range(n // P):
                            t0 = tt * P
                            last = mm(acc(d, t0, t0 + P), kin[64 * d:64 * d + DK, t0:t0 + P], qr[64 * d:64 * d + DK, t0:t0 + P], start=True, stop=True)
                        last.then_inc(a_done, 1)
                    for c in range(NCH):
                        r = 64 * (c % 2)
                        last = mm(ps[:, u_col(c):u_col(c) + DV], ktok[r:r + 64, c // 2, :], vtok[r:r + 64, c // 2, h * DV:(h + 1) * DV], start=True, stop=True)
                    last.then_inc(ud_done, 1)
                    pe.wait_ge(am_ready, 2 * hh + 2)
                    pe.wait_ge(st_ready, hh + 1)
                    for tt in range(n // P):
                        o = (tt * P, (tt + 1) * P)
                        for d in range(2):
                            mm(acc(1, *o, (0, DV)), vtok[:, tt, h * DV:(h + 1) * DV],
                               am[d][:, tt * P:(tt + 1) * P], start=(d == 0), stop=False)
                        for j in range(2):
                            c = 2 * tt + j
                            last = mm(acc(1, c * CHUNK, (c + 1) * CHUNK, (0, DV)), st[:, c, :], qr[:, c * CHUNK:(c + 1) * CHUNK],
                                      start=False, stop=(j == 1))
                    last.then_inc(go_done, 1)
                    pe.wait_ge(osq_ready, hh + 1)
                    for a, b in chunks(n):
                        last = mm(acc(2, a, b, (0, DV)), ones[0:DV, 0:DV], osq[0:DV, a:b], start=True, stop=True)
                    last.then_inc(ossq_done, 1)
                barrier()

                pe.wait_ge(mlo_ready, (l + 1) * KOUT)
                for u in range(KD):
                    pe.wait_ge(lo_ready, s_base(l) + S_OUT + u + 1)
                    if u >= 4:
                        pe.wait_ge(x_upd, l * KD * 4 + u - 3)
                    product(u % 4, u % 2, mhi, mlo, [P] * 5 + [DV] * 4, n)

                pe.wait_ge(x_upd, l * KD * 4 + KD)
                sum_squares(2 * l + 1, n)
                pe.wait_ge(h_ready, (2 * l + 2) * KD)
                for p, np_ in enumerate(PARTS):
                    s0, p0 = s_base(l) + s_up(p), pair_base(l, p)
                    xu = l * KD * 4 + (1 + p) * KD

                    def up_pair(s_at, free, s):
                        for ab in range(2):
                            pe.wait_ge(lo_ready, s_at + (2 * s + ab + 1))
                            if ab == 0:
                                free()
                            product(2 * s + ab, ab, hhi, hlo, [P] * KD, n)

                    for s in range(2):
                        up_pair(s0, lambda: pe.wait_ge(x_upd, xu), s)
                    with pe.Fori(1, np_ // 2) as it:
                        for s in range(2):
                            up_pair(it * 4 + s0, lambda: pe.wait_ge(side_ready, it * 2 + (p0 + s - 1)), s)
                    pe.wait_ge(side_ready, p0 + np_)
                    pe.wait_ge(hid_ready, p0 + np_)
                    for u in range(KD):
                        pe.wait_ge(lo_ready, s0 + 2 * np_ + u + 1)
                        if u >= 4:
                            pe.wait_ge(x_upd, xu + u - 3)
                        product(u % 4, u % 2, fhi, flo, [P] * np_, n)

        @block.scalar
        def _(act):
            A = nc.scalar.activation
            copy = nc.scalar.copy
            me = Chain(act, act_step)
            bar = [0]

            def barrier():
                bar[0] += 1
                nc.scalar.drain().then_inc(act_bar, 1)
                act.wait_ge(pe_bar, bar[0])
                act.wait_ge(dve_bar, bar[0])

            def high(g, n, w):
                act.wait_ge(raw_in[g % RING], 16 * (g // RING + 1))
                if n >= SPLIT:
                    act.wait_ge(unit_done, n - 1)
                copy(whi[n % SPLIT][:, 0:w], raw[g % RING][:, 0:w]).then_inc(hi_ready, 1)

            def inverse_rms(out_, in_, count, done):
                rows = out_.shape[0]
                me.step(A(out_, in_, ACT.Ln, bias=eps[0:rows, :], scale=1.0 / count))
                me.wait()
                A(out_, out_, ACT.Exp, scale=-0.5).then_inc(done, 1)

            def norm(l, which, n):
                nn = 2 * l + which
                if nn == 0:
                    act.wait_ge(x_in, 16 * KD)
                elif which == 0:
                    act.wait_ge(x_upd, l * KD * 4)
                for k in range(KD):
                    if which == 1:
                        act.wait_ge(x_upd, l * KD * 4 + k + 1)
                    if k >= 2:
                        act.wait_ge(ssq_done, nn * KD + k - 1)
                    A(sq[k % 2][:, 0:n], xt[:, k, 0:n], ACT.Square).then_inc(sq_ready, 1)
                act.wait_ge(ssq_done, (nn + 1) * KD)
                inverse_rms(rstd[:, 0:n], acc(0, 0, n), D, rstd_ready)
                act.wait_ge(mod_ready, 2 * l + 1 + which)
                for k in range(KD):
                    act.wait_ge(xn_ready, nn * KD + k + 1)
                    if k >= 2:
                        act.wait_ge(h_ready, nn * KD + k - 1)
                    for a, b, c in streams(n):
                        me.step(A(hf[k % 2][:, a:b], xn[k % 2][:, a:b], ACT.Identity,
                                  bias=modv[:, 3 * which * KD + k, c:c + 1], scale=mscale[:, which, k, c:c + 1]))
                    me.wait()
                    copy(hhi[:, k, 0:n], hf[k % 2][:, 0:n]).then_inc(hh_ready, 1)

            act.wait_ge(const_in, 16 * NCONST)
            act.wait_ge(table_in, 16 * NTABLE)
            act.wait_ge(ready0, 1)
            A(csil[:], craw[:], ACT.Silu).then_inc(csil_ready, 1)
            for l in range(DEPTH):
                n = width(l)
                sb, rb = s_base(l), raw_base(l)
                norm(l, 0, NT if l == 0 else NT)

                g0 = rb + NMOD
                for u in range(2):
                    high(g0 + u, sb + u, KD * P)
                for u in range(INP_UNITS):
                    if u + 2 < INP_UNITS:
                        high(g0 + u + 2, sb + u + 2, KD * P)
                    if u % 2 and u < U_G0:
                        continue
                    act.wait_ge(unit_done, sb + u + 1)
                    s = u % 4
                    if u == U_CQ0:
                        copy(lr[0:RANK, :], acc(s, 0, NT, (QH, QH + RANK)))
                        ins = copy(cq[:, 0, :], acc(s, 0, NT, (0, QH)))
                    elif u == U_CKV:
                        ins = copy(ckv[:], acc(s))
                    elif u == U_K23:
                        ins = copy(kp[:, 1, :], acc(s))
                    elif u == U_V1:
                        ins = copy(vt[:, 1, :], acc(s))
                    elif u == U_F0:
                        ins = copy(ft[:, 0, 0:n], acc(s, 0, n))
                    elif u == U_Q01:
                        ins = nc.scalar.mul(qp[:, 0, 0:n], acc(s, 0, n), DK ** -0.5)
                    else:
                        ins = A(gs[0:DV, u - U_G0, 0:n], acc(s, 0, n, (0, DV)), ACT.Silu)
                    ins.then_inc(evac_a, 1)
                barrier()

                for tt in range(1, 6, 2):
                    act.wait_ge(vtr_done, 6 * l + tt + 1)
                    copy(vtok[:, tt, :], bank(tt, 0, GH * DV)).then_inc(vtr_a, 1)
                for tt in range(1, n // P, 2):
                    act.wait_ge(gd_done, 6 * l + tt + 1)
                    copy(gdft[:, tt, :], bank(6 + tt % 2)).then_inc(gd_a, 1)
                act.wait_ge(whole_used, w_base(l) + NMOD + 4)
                copy(mixfa[:, 0, 0:NX], bank(0))
                barrier()

                A(qsq[0][0:QH, :], cq[:, 0, :], ACT.Square).then_inc(lat_sq, 1)
                A(qsq[1][0:QH, :], cq[:, 1, :], ACT.Square).then_inc(lat_sq, 1)
                A(ksq[:], ckv[:], ACT.Square).then_inc(lat_sq, 1)
                act.wait_ge(lat_ssq, 2 * l + 1)
                inverse_rms(rsq[0:QH, :], acc(0, 0, NT, (0, QH)), Q_LORA, lat_rs)
                act.wait_ge(lat_ssq, 2 * l + 2)
                inverse_rms(rsk[:], acc(1), KV_LORA, lat_rs)
                A(ksq[NOPE:QK, :], kpe[NOPE:QK, :], ACT.Square).then_inc(kpe_sq, 1)
                for tt in range(1, 6, 2):
                    act.wait_ge(va_done, 6 * l + tt + 1)
                    copy(vall[:, tt, :], bank(6 + tt % 2, 0, HEADS * VDIM)).then_inc(va_a, 1)
                for h in range(HEADS):
                    hh = l * HEADS + h
                    act.wait_ge(qk_done, 2 * hh + 1)
                    A(qsq[0][0:QK, 0:n], acc(0, 0, n, (0, QK)), ACT.Square).then_inc(qksq_ready, 1)
                    act.wait_ge(qk_done, 2 * hh + 2)
                    A(ksq[0:NOPE, :], acc(1, 0, NT, (0, NOPE)), ACT.Square).then_inc(qksq_ready, 1)
                    act.wait_ge(qkssq_done, 2 * hh + 1)
                    inverse_rms(rsq[0:QK, 0:n], acc(2, 0, n, (0, QK)), QK, qkrs_ready)
                    act.wait_ge(qkssq_done, 2 * hh + 2)
                    inverse_rms(rsk[0:QK, :], acc(3, 0, NT, (0, QK)), QK, qkrs_ready)
                    ub, units = u_base(l, h), attn_units(l)

                    def exp_of(j):
                        kind, _ = units[j]
                        a, b = (0, NT) if kind == "x" else (NX, NT)
                        slot = (j if kind == "x" else j + 1) % 2
                        act.wait_ge(mx_ready, ub + j + 1)
                        if ub + j >= 2:
                            act.wait_ge(t_done, ub + j - 1)
                        A(pr[j % 2][:, a:b], acc(slot, a, b), ACT.Exp, bias=nmx[:, j % 2:j % 2 + 1], scale=SCALE,
                          accum_out=rsum[:, j % 2:j % 2 + 1]).then_inc(p_exp, 1)

                    def pt_out(j):
                        kind, q0 = units[j]
                        act.wait_ge(t_done, ub + j + 1)
                        if kind == "x":
                            if j == 0 and h:
                                act.wait_ge(pv_done, o_base(l, h - 1) + 1)
                            copy(ptx[:, 0:4, q0:q0 + P], acc(2 + j % 2, 0, 4 * P).rearrange("p (k q) -> p k q", k=4)).then_inc(pt_a, 1)
                        else:
                            if j == 4 and h:
                                act.wait_ge(pv_done, o_base(l, h))
                            copy(ptc[:, :, q0 - NX:q0 - NX + P], acc(2 + j % 2, 0, 2 * P).rearrange("p (k q) -> p k q", k=2)).then_inc(pt_a, 1)

                    exp_of(0)
                    exp_of(1)
                    for j in range(4):
                        pt_out(j)
                        if j + 2 < 4:
                            exp_of(j + 2)
                    if l < DEPTH - 1:
                        exp_of(4)
                        exp_of(5)
                        pt_out(4)
                        pt_out(5)
                barrier()

                for i in range(3):
                    act.wait_ge(z_done, 6 * l + 2 * i + 2)
                    if i:
                        act.wait_ge(g_ready, 3 * l + i)
                    me.step(A(ga[:], ps[:, i * 1024:(i + 1) * 1024], ACT.Abs))
                    me.wait()
                    me.step(A(ga[:], ga[:], ACT.Exp, scale=-1.0))
                    me.wait()
                    A(ga[:], ga[:], ACT.Ln, bias=ones[:, 0:1]).then_inc(ls_ready, 1)
                for h in range(GH):
                    hh = l * GH + h
                    act.wait_ge(eo_raw, hh + 1)
                    A(e_pos[:], acc(0), ACT.Exp).then_inc(e_ready, 1)
                    A(e_neg[:], acc(0), ACT.Exp, scale=-1.0).then_inc(e_ready, 1)
                    A(decay[:], blast[:], ACT.Exp).then_inc(e_ready, 1)
                    A(e_out[:], e_out[:], ACT.Exp).then_inc(e_ready, 1)
                    act.wait_ge(kt_done, hh + 1)
                    copy(ktok[:].rearrange("p a b -> p (a b)"), acc(1)).then_inc(ktok_ready, 1)
                    act.wait_ge(go_done, hh + 1)
                    A(osq[0:DV, 0:n], acc(1, 0, n, (0, DV)), ACT.Square).then_inc(osq_ready, 1)
                    act.wait_ge(ossq_done, hh + 1)
                    inverse_rms(ors[0:DV, 0:n], acc(2, 0, n, (0, DV)), DV, ors_ready)
                barrier()

                g0, n0 = rb + NMOD + INP_UNITS + four_tiles(l), sb + S_OUT
                high(g0, n0, KOUT * P)
                for m in range(KOUT):
                    if m < 5:
                        copy(mhi[:, m, 0:n], mixfa[:, m, 0:n]).then_inc(mhi_ready, 1)
                    else:
                        copy(mhi[0:DV, m, 0:n], gs[0:DV, m - 5, 0:n]).then_inc(mhi_ready, 1)
                    if m == 0:
                        high(g0 + 1, n0 + 1, KOUT * P)
                for i in range(2, KD + 2):
                    high(g0 + i, n0 + i, KOUT * P if i < KD else KD * P)

                norm(l, 1, n)
                for p, np_ in enumerate(PARTS):
                    i0 = s_up(p) - S_OUT
                    p0 = pair_base(l, p)

                    def round_(it):
                        q_at = p0 if it is None else it * 2 + p0
                        for s in range(2):
                            for ab, c in ((0, ca), (1, cb)):
                                i = 2 * s + ab
                                g = g0 + i0 + i + 2
                                act.wait_ge(raw_in[g % RING], 16 * (g // RING + 1) if it is None else it * 16 + 16 * (g // RING + 1))
                                done = n0 + i0 + i + 1
                                act.wait_ge(unit_done, done if it is None else it * 4 + done)
                                copy(whi[ab][:, 0:KD * P], raw[g % RING][:, 0:KD * P]).then_inc(hi_ready, 1)
                                if ab == 0 and (it is not None or p0 > 0):
                                    act.wait_ge(fh_ready, q_at + (s - 1))
                                col = V_CONV + (sum(PARTS[:p]) + s) * 8 + 4 * ab
                                w1, b0 = [par[:, l, col + o:col + o + 1] if it is None else par[:, l, bass.ds(it * 16 + (col + o), 1)]
                                          for o in (1, 3)]
                                A(c[s][:, 0:n], acc(i, 0, n), ACT.Identity, bias=b0, scale=w1).then_inc(center_ready, 1)
                            act.wait_ge(gate_ready, q_at + (s + 1))
                            A(ca[s][:, 0:n], ca[s][:, 0:n], ACT.Silu).then_inc(silu_ready, 1)
                            act.wait_ge(fh_ready, q_at + (s + 1))
                            to = fhi[:, s:s + 1, 0:n] if it is None else fhi[:, bass.ds(it * 2 + s, 1), 0:n]
                            copy(to, cf[s][:, 0:n].rearrange("p (a b) -> p a b", a=1)).then_inc(hidh_ready, 1)

                    round_(None)
                    with act.Fori(1, np_ // 2) as it:
                        round_(it)
                    for u in range(KD):
                        i = i0 + 2 * np_ + u + 2
                        if u + 2 < KD:
                            high(g0 + i, n0 + i, np_ * P)
                        elif p < len(PARTS) - 1:
                            high(g0 + i, n0 + i, KD * P)

        @block.vector
        def _(dve):
            stt, tt_, ts = nc.vector.scalar_tensor_tensor, nc.vector.tensor_tensor, nc.vector.tensor_scalar
            copy = nc.vector.tensor_copy
            me = Chain(dve, dve_step)
            bar = [0]

            def barrier():
                bar[0] += 1
                nc.vector.drain().then_inc(dve_bar, 1)
                dve.wait_ge(pe_bar, bar[0])
                dve.wait_ge(act_bar, bar[0])

            def low(g, n, w):
                dve.wait_ge(hi_ready, n + 1)
                tt_(wlo[n % SPLIT][:, 0:w], raw[g % RING][:, 0:w], whi[n % SPLIT][:, 0:w].bitcast(F32), ALU.subtract).then_inc(lo_ready, 1)

            def norm(l, which, n):
                nn = 2 * l + which
                dve.wait_ge(rstd_ready, nn + 1)

                def low_h(k):
                    dve.wait_ge(hh_ready, nn * KD + k + 1)
                    tt_(hlo[:, k, 0:n], hf[k % 2][:, 0:n], hhi[:, k, 0:n].bitcast(F32), ALU.subtract).then_inc(h_ready, 1)

                for k in range(KD):
                    if k >= 2:
                        dve.wait_ge(hh_ready, nn * KD + k - 1)
                    tt_(xn[k % 2][:, 0:n], xt[:, k, 0:n], rstd[:, 0:n], ALU.mult).then_inc(xn_ready, 1)
                    if k:
                        low_h(k - 1)
                low_h(KD - 1)

            def modulation(l, half):
                first, cnt = (0, MOD_A) if half == 0 else (MOD_A, MOD_B)
                dve.wait_ge(whole_used, w_base(l) + (MOD_A if half == 0 else NMOD))
                src = bank(6 + half, 0, 2 * cnt).rearrange("p (a b) -> p a b", b=2)
                bias = par[:, l, V_MODB + first:V_MODB + first + cnt].unsqueeze(2).to_broadcast([P, cnt, 2])
                me.step(tt_(modv[:, first:first + cnt, :], src, bias, ALU.add))
                me.wait()
                sc = modv[:, (3 * half + 1) * KD:(3 * half + 2) * KD, :]
                v = V_N2 if half else V_N1
                nw = par[:, l, v:v + KD].unsqueeze(2).to_broadcast([P, KD, 2])
                stt(mscale[:, half, :, :], sc, 1.0, nw, ALU.add, ALU.mult).then_inc(mod_ready, 1)

            def update(l, k, s, gate, v, n):
                if v >= KD:
                    dve.wait_ge(x_upd, v - KD + 1)
                for a, b, c in streams(n):
                    last = stt(xt[:, k, a:b], acc(s, a, b), modv[:, gate * KD + k, c:c + 1], xt[:, k, a:b], ALU.mult, ALU.add)
                last.then_inc(x_upd, 1)

            nc.vector.memset(ones[:], 1.0)
            nc.vector.memset(eps[:], EPS).then_inc(ready0, 1)
            dve.wait_ge(const_in, 16 * NCONST)
            dve.wait_ge(table_in, 16 * NTABLE)
            dve.wait_ge(x_in, 16 * KD)
            for l in range(DEPTH):
                n = width(l)
                sb, rb = s_base(l), raw_base(l)
                modulation(l, 0)
                if l:
                    dve.wait_ge(x_upd, l * KD * 4)
                nc.vector.memset(lr[:], 1.0)
                norm(l, 0, NT)
                modulation(l, 1)

                g0 = rb + NMOD
                for u in range(2):
                    low(g0 + u, sb + u, KD * P)
                for u in range(INP_UNITS):
                    if u + 2 < INP_UNITS:
                        low(g0 + u + 2, sb + u + 2, KD * P)
                    if u % 2 == 0 or u >= U_G0:
                        continue
                    dve.wait_ge(unit_done, sb + u + 1)
                    s = u % 4
                    if u == U_CQ1:
                        copy(kpe[NOPE:QK, :], acc(s, 0, NT, (QH, P)))
                        ins = copy(cq[:, 1, :], acc(s, 0, NT, (0, QH)))
                    elif u == U_K01:
                        ins = copy(kp[:, 0, :], acc(s))
                    elif u in (U_V0, U_V2):
                        ins = copy(vt[:, u - U_V0, :], acc(s))
                    elif u == U_F1:
                        ins = copy(ft[:, 1, 0:n], acc(s, 0, n))
                    else:
                        ins = ts(qp[:, 1, 0:n], acc(s, 0, n), DK ** -0.5, None, ALU.mult)
                    ins.then_inc(evac_d, 1)
                barrier()

                for tt in range(0, 6, 2):
                    dve.wait_ge(vtr_done, 6 * l + tt + 1)
                    copy(vtok[:, tt, :], bank(tt, 0, GH * DV)).then_inc(vtr_d, 1)
                for tt in range(0, n // P, 2):
                    dve.wait_ge(gd_done, 6 * l + tt + 1)
                    copy(gdft[:, tt, :], bank(6 + tt % 2)).then_inc(gd_d, 1)
                dve.wait_ge(whole_used, w_base(l) + NMOD + 4)
                copy(mixfa[:, 1, 0:NX], bank(1))
                if l < DEPTH - 1:
                    dve.wait_ge(whole_used, w_base(l) + NMOD + 8)
                    copy(mixfa[:, 0:2, NX:NT], bank(2).rearrange("p (f t) -> p f t", f=2))
                barrier()

                dve.wait_ge(lat_rs, 2 * l + 1)
                for j in range(2):
                    last = stt(cq[:, j, :], cq[:, j, :], par[0:QH, l, V_QL + j:V_QL + j + 1], rsq[0:QH, :], ALU.mult, ALU.mult)
                last.then_inc(lat_n, 1)
                dve.wait_ge(lat_rs, 2 * l + 2)
                stt(ckv[:], ckv[:], par[:, l, V_KVL:V_KVL + 1], rsk[:], ALU.mult, ALU.mult).then_inc(lat_n, 1)
                dve.wait_ge(kpe_sq, l + 1)
                kw = par[:, l, V_KW:V_KW + 1]
                ts(kpe[NOPE:QK, :], kpe[NOPE:QK, :], kw[NOPE:QK, :], None, ALU.mult).then_inc(kpw_ready, 1)
                dve.wait_ge(kpe_rot, l + 1)
                kx = kpe[NOPE:QK, 0:NX]
                me.step(tt_(rtmp[NOPE:QK, :], acc(2, 0, NX, (NOPE, QK)), rope[NOPE:QK, 1, :], ALU.mult))
                me.step(tt_(kx, kx, rope[NOPE:QK, 0, :], ALU.mult))
                me.wait()
                me.step(tt_(kx, kx, rtmp[NOPE:QK, :], ALU.add))
                for tt in range(0, 6, 2):
                    dve.wait_ge(va_done, 6 * l + tt + 1)
                    copy(vall[:, tt, :], bank(6 + tt % 2, 0, HEADS * VDIM)).then_inc(va_d, 1)
                me.wait()
                for h in range(HEADS):
                    hh = l * HEADS + h
                    q_, k_ = qh[h % 2], kh[h % 2]
                    dve.wait_ge(qkrs_ready, 2 * hh + 1)
                    stt(q_[:, 0:n], acc(0, 0, n, (0, QK)), par[0:QK, l, V_QW:V_QW + 1], rsq[0:QK, 0:n], ALU.mult, ALU.mult).then_inc(qn_ready, 1)
                    dve.wait_ge(qkrs_ready, 2 * hh + 2)
                    stt(k_[0:NOPE, :], acc(1, 0, NT, (0, NOPE)), kw[0:NOPE, :], rsk[0:NOPE, :], ALU.mult, ALU.mult)
                    tt_(k_[NOPE:QK, :], kpe[NOPE:QK, :], rsk[NOPE:QK, :], ALU.mult)
                    dve.wait_ge(qrot_done, hh + 1)
                    qx = q_[NOPE:QK, 0:NX]
                    me.step(tt_(rtmp[NOPE:QK, :], acc(2, 0, NX, (NOPE, QK)), rope[NOPE:QK, 1, :], ALU.mult))
                    me.step(tt_(qx, qx, rope[NOPE:QK, 0, :], ALU.mult))
                    me.wait()
                    tt_(qx, qx, rtmp[NOPE:QK, :], ALU.add).then_inc(qk_ready, 1)
                    ub, units = u_base(l, h), attn_units(l)

                    def row_max(j):
                        kind, _ = units[j]
                        a, b = (0, NT) if kind == "x" else (NX, NT)
                        dve.wait_ge(s_done, ub + j + 1)
                        me.step(nc.vector.reduce_max(mx[:, j % 2:j % 2 + 1], acc((j if kind == "x" else j + 1) % 2, a, b), AX_X))
                        me.wait()
                        ts(nmx[:, j % 2:j % 2 + 1], mx[:, j % 2:j % 2 + 1], -SCALE, None, ALU.mult).then_inc(mx_ready, 1)

                    def divide(j):
                        kind, _ = units[j]
                        a, b = (0, NT) if kind == "x" else (NX, NT)
                        dve.wait_ge(p_exp, ub + j + 1)
                        me.step(nc.vector.reciprocal(rinv[:, j % 2:j % 2 + 1], rsum[:, j % 2:j % 2 + 1]))
                        me.wait()
                        ts(pr[j % 2][:, a:b], pr[j % 2][:, a:b], rinv[:, j % 2:j % 2 + 1], None, ALU.mult).then_inc(p_ready, 1)

                    def pt_out(j):
                        q0 = units[j][1]
                        dve.wait_ge(t_done, ub + j + 1)
                        if j == 0 and h:
                            dve.wait_ge(pv_done, o_base(l, h - 1) + 1)
                        copy(ptx[:, 4:6, q0:q0 + P], acc(2 + j % 2, 4 * P, 6 * P).rearrange("p (k q) -> p k q", k=2)).then_inc(pt_d, 1)

                    row_max(0)
                    row_max(1)
                    divide(0)
                    for j in range(4):
                        pt_out(j)
                        if j + 2 < 4:
                            row_max(j + 2)
                        if j + 1 < 4:
                            divide(j + 1)
                    r0 = VDIM * (h % 2)
                    dve.wait_ge(pv_done, o_base(l, h) + 1)
                    copy(mixfa[r0:r0 + VDIM, 2 + h // 2, 0:NX], acc(0, 0, NX, (0, VDIM))).then_inc(o_out, 1)
                    if l < DEPTH - 1:
                        row_max(4)
                        row_max(5)
                        divide(4)
                        divide(5)
                        dve.wait_ge(pv_done, o_base(l, h) + 2)
                        copy(mixfa[r0:r0 + VDIM, 2 + h // 2, NX:NT], acc(1, 0, NC, (0, VDIM))).then_inc(o_out, 1)
                barrier()

                for t in (qr, kr, am[0], am[1]):
                    me.step(nc.vector.memset(t[:], 0.0))
                me.step(nc.vector.memset(st[:].rearrange("p a b -> p (a b)"), 0.0))
                for i in range(3):
                    dve.wait_ge(ls_ready, 3 * l + i + 1)
                    stt(gtok[:, 2 * i:2 * i + 2, :].rearrange("p a b -> p (a b)"), ps[:, i * 1024:(i + 1) * 1024], 0.0, ga[:],
                        ALU.min, ALU.subtract).then_inc(g_ready, 1)
                me.wait()
                fwd = [8, 9, 10, 11, 0, 1, 2, 3, 4, 5, 6, 7]
                bwd = [11, 10, 9, 8, 7, 6, 5, 4, 3, 2, 1, 0]
                for h in range(GH):
                    hh = l * GH + h
                    src = 64 * (h % 2)
                    for d in range(2):
                        me.step(copy(qr[64 * d:64 * d + DK, 0:n], qp[src:src + DK, h // 2, 0:n]))
                        me.step(copy(kr[64 * d:64 * d + DK, :], kp[src:src + DK, h // 2, :]))
                    dve.wait_ge(b_done, hh + 1)
                    for d, t in ((0, CHUNK - 1), (1, 0)):
                        rows = (64 * d, 64 * d + 64)
                        me.step(copy(blast[rows[0]:rows[1], :], acc(0, 0, NT, rows).rearrange("p (c t) -> p c t", t=CHUNK)[:, :, t]))
                    me.wait()
                    tt_(e_out[:].rearrange("p (c t) -> p c t", t=CHUNK), blast[:].unsqueeze(2).to_broadcast([P, NCH, CHUNK]),
                        acc(0).rearrange("p (c t) -> p c t", t=CHUNK), ALU.subtract).then_inc(eo_raw, 1)
                    dve.wait_ge(e_ready, 4 * hh + 2)
                    me.step(tt_(kin[:], kr[:], e_neg[:], ALU.mult))
                    tt_(qr[:, 0:n], qr[:, 0:n], e_pos[:, 0:n], ALU.mult).then_inc(gq_ready, 1)
                    dve.wait_ge(e_ready, 4 * hh + 4)
                    tt_(kr[:], kr[:], e_out[:], ALU.mult).then_inc(gk_ready, 1)
                    for d in range(2):
                        dve.wait_ge(a_done, 2 * hh + d + 1)
                        for t in range(n // P):
                            last = nc.vector.copy_predicated(am[d][:, t * P:(t + 1) * P], amask[:, d, :], acc(d, t * P, (t + 1) * P))
                        last.then_inc(am_ready, 1)
                    dve.wait_ge(ud_done, hh + 1)
                    for i in range(NCH - 1):
                        for d, order in ((0, fwd), (1, bwd)):
                            a, b = order[i], order[i + 1]
                            r = slice(64 * d, 64 * d + 64)
                            u = ps[r, u_col(a):u_col(a) + DV]
                            if i:
                                me.wait(1)
                            ins = stt(st[r, b, :], st[r, a, :], decay[r, a:a + 1], u, ALU.mult, ALU.add)
                            if i == NCH - 2 and d == 1:
                                ins.then_inc(st_ready, 1)
                            else:
                                me.step(ins)
                    dve.wait_ge(ors_ready, hh + 1)
                    me.step(stt(ot[0:DV, 0:n], acc(1, 0, n, (0, DV)), par[0:DV, l, V_GN:V_GN + 1], ors[0:DV, 0:n], ALU.mult, ALU.mult))
                    me.wait()
                    tt_(gs[0:DV, h, 0:n], gs[0:DV, h, 0:n], ot[0:DV, 0:n], ALU.mult).then_inc(lin_ready, 1)
                barrier()

                g0, n0 = rb + NMOD + INP_UNITS + four_tiles(l), sb + S_OUT
                low(g0, n0, KOUT * P)
                for m in range(KOUT):
                    dve.wait_ge(mhi_ready, l * KOUT + m + 1)
                    rows, src = (P, mixfa[:, m, 0:n]) if m < 5 else (DV, gs[0:DV, m - 5, 0:n])
                    tt_(mlo[0:rows, m, 0:n], src, mhi[0:rows, m, 0:n].bitcast(F32), ALU.subtract).then_inc(mlo_ready, 1)
                    if m == 0:
                        low(g0 + 1, n0 + 1, KOUT * P)
                for u in range(KD):
                    low(g0 + u + 2, n0 + u + 2, KOUT * P if u + 2 < KD else KD * P)
                    dve.wait_ge(unit_done, n0 + u + 1)
                    update(l, u, u % 4, 2, l * KD * 4 + u, n)

                norm(l, 1, n)
                for p, np_ in enumerate(PARTS):
                    i0 = s_up(p) - S_OUT
                    p0 = pair_base(l, p)

                    def round_(it):
                        q_at = p0 if it is None else it * 2 + p0
                        for s in range(2):
                            for ab, c in ((0, ca), (1, cb)):
                                i = 2 * s + ab
                                g = g0 + i0 + i + 2
                                hi = n0 + i0 + i + 3
                                dve.wait_ge(hi_ready, hi if it is None else it * 4 + hi)
                                tt_(wlo[ab][:, 0:KD * P], raw[g % RING][:, 0:KD * P], whi[ab][:, 0:KD * P].bitcast(F32), ALU.subtract).then_inc(lo_ready, 1)
                                dve.wait_ge(center_ready, 2 * q_at + (2 * s + ab + 1))
                                col = V_CONV + (sum(PARTS[:p]) + s) * 8 + 4 * ab
                                w0, w2 = [par[:, l, col + o:col + o + 1] if it is None else par[:, l, bass.ds(it * 16 + (col + o), 1)]
                                          for o in (0, 2)]
                                parts = streams(n)
                                for a, b, _ in parts:
                                    me.step(stt(c[s][:, a + 1:b], acc(i, a, b - 1), w0, c[s][:, a + 1:b], ALU.mult, ALU.add))
                                for a, b, _ in parts:
                                    me.wait(len(parts) - 1)
                                    ins = stt(c[s][:, a:b - 1], acc(i, a + 1, b), w2, c[s][:, a:b - 1], ALU.mult, ALU.add)
                                    if b == parts[-1][1]:
                                        ins.then_inc(side_ready if ab else gate_ready, 1)
                                    else:
                                        me.step(ins)
                            dve.wait_ge(silu_ready, q_at + (s + 1))
                            dve.wait_ge(side_ready, q_at + (s + 1))
                            tt_(cf[s][:, 0:n], ca[s][:, 0:n], cb[s][:, 0:n], ALU.mult).then_inc(fh_ready, 1)
                            dve.wait_ge(hidh_ready, q_at + (s + 1))
                            h_, l_ = [t[:, s:s + 1, 0:n] if it is None else t[:, bass.ds(it * 2 + s, 1), 0:n] for t in (fhi, flo)]
                            tt_(l_, cf[s][:, 0:n].rearrange("p (a b) -> p a b", a=1), h_.bitcast(F32), ALU.subtract).then_inc(hid_ready, 1)

                    before = me.n
                    round_(None)
                    each = me.n - before
                    before = me.n
                    with dve.Fori(1, np_ // 2) as it:
                        me.off = it * each - each
                        round_(it)
                        me.off = None
                    me.n = before + each * (np_ // 2 - 1)
                    for u in range(KD):
                        i = i0 + 2 * np_ + u + 2
                        if u + 2 < KD:
                            low(g0 + i, n0 + i, np_ * P)
                        elif p < len(PARTS) - 1:
                            low(g0 + i, n0 + i, KD * P)
                        dve.wait_ge(unit_done, n0 + i0 + 2 * np_ + u + 1)
                        update(l, u, u % 4, 5, l * KD * 4 + (1 + p) * KD + u, n)


def _tiles(w, cols):
    cols = np.asarray(cols)
    rows = w.shape[1]
    padded = np.concatenate([w, np.zeros(w.shape[:2] + (1,), w.dtype)], axis=2)[:, :, cols.reshape(-1)]
    t = padded.reshape(DEPTH, rows // P, P, cols.shape[0], P)
    return np.ascontiguousarray(t.transpose(0, 3, 2, 1, 4).reshape(DEPTH, cols.shape[0], P, rows))


def _in_columns():
    m0, g0 = F_WIDTH, F_WIDTH + Q_LORA + KV_LORA + ROPE
    q0, k0, v0 = g0, g0 + GH * DK, g0 + 2 * GH * DK
    r0, o0 = v0 + GH * DV, v0 + GH * DV + RANK

    def span(a, n, pad=0):
        return list(range(a, a + n)) + [-1] * pad

    u = [span(m0, QH) + span(r0, RANK, 16),
         span(m0 + QH, QH) + span(m0 + Q_LORA + KV_LORA, ROPE),
         span(m0 + Q_LORA, KV_LORA)]
    u += [span(k0 + 2 * i * DK, DK, 16) + span(k0 + (2 * i + 1) * DK, DK, 16) for i in range(2)]
    u += [span(v0 + i * P, P) for i in range(3)]
    u += [span(i * P, P) for i in range(2)]
    u += [span(q0 + 2 * i * DK, DK, 16) + span(q0 + (2 * i + 1) * DK, DK, 16) for i in range(2)]
    u += [span(o0 + h * DV, DV, P - DV) for h in range(GH)]
    return u


def _dft(n, block):
    t = np.arange(n)
    ang = 2 * np.pi * (np.outer(t, t) % n) / n
    norm = 1 / np.sqrt(n * F_DIM)
    cs = np.stack([np.cos(ang), -np.sin(ang)], 1) * norm
    cs = cs.reshape(n // P, P, 2, n // block, block).transpose(3, 1, 0, 2, 4)
    return np.ascontiguousarray(cs.reshape(n // block, P, -1)).astype(np.float32)


def _constants():
    s, t = np.arange(P)[:, None], np.arange(P)[None, :]
    same = s // CHUNK == t // CHUNK
    order = [same & (s <= t), same & (s >= t)]
    tri = np.stack(order, 1).astype(np.float32) / GATE_NORM
    mask = np.concatenate(order, 1).astype(np.int32)
    half = ROPE // 2
    inv = ROPE_BASE ** (-np.arange(0, half, 2) / half)
    pos = np.arange(NX)
    ang = [np.outer(inv, pos // GRID_W), np.outer(inv, pos % GRID_W)]
    ang = np.concatenate([ang[0], ang[0], ang[1], ang[1]])
    rot = np.zeros((ROPE, ROPE), np.float32)
    for b in (0, half):
        for i in range(half // 2):
            rot[b + half // 2 + i, b + i] = -1
            rot[b + i, b + half // 2 + i] = 1
    f = np.arange(F_DIM)
    a = 2 * np.pi * np.outer(f, f) / F_DIM
    dft = np.concatenate([np.kron(np.eye(2), np.cos(a)), np.kron(np.eye(2), np.sin(a))], 1)
    return {
        "k_ident": np.eye(P, dtype=np.float32), "k_tri": tri.reshape(P, -1), "k_mask": mask,
        "k_rope": np.concatenate([np.cos(ang), np.sin(ang)], 1).astype(np.float32), "k_rot": rot,
        "k_dft": dft.astype(np.float32), "w_four_x": _dft(NX, P), "w_four_c": _dft(NC, CHUNK),
    }


def _rows(v, rows=P):
    t = v.reshape(DEPTH, -1, rows).transpose(0, 2, 1)
    return np.concatenate([t, np.zeros((DEPTH, P - rows, t.shape[2]), v.dtype)], 1)


def _layout(i):
    x = np.concatenate([i["x"][0], i["ctx"][0]], 0)
    conv = np.concatenate([i["ffn_conv_w"], i["ffn_conv_b"][:, None]], 1)
    conv = conv.reshape(DEPTH, 4, 2, NPAIR, P).transpose(0, 4, 3, 2, 1).reshape(DEPTH, P, NPAIR * 8)
    vec = np.concatenate([
        _rows(i["mod_b"]), _rows(i["norm1_w"]), _rows(i["norm2_w"]), _rows(i["mla_q_lora_norm_w"], QH),
        _rows(i["mla_kv_lora_norm_w"]), _rows(i["mla_q_norm_w"], QK), _rows(i["mla_k_norm_w"], QK),
        _rows(i["gla_norm_w"], DV), conv], 2)
    wo = i["w_out"]
    blocks = [wo[:, k * P:(k + 1) * P] for k in range(5)]
    blocks += [np.concatenate([wo[:, 5 * P + h * DV:5 * P + (h + 1) * DV], np.zeros((DEPTH, P - DV, D), wo.dtype)], 1) for h in range(GH)]
    up = np.arange(2 * D_FF).reshape(2, NPAIR, P).transpose(1, 0, 2).reshape(2 * NPAIR, P)
    cols = np.arange(D).reshape(KD, P)
    kv = np.arange(HEADS * (NOPE + VDIM)).reshape(HEADS, -1)
    gk = np.zeros((DEPTH, RANK + 1, GH, 2, 64), np.float32)
    for d, s in enumerate(("fwd", "bwd")):
        gk[:, :RANK, :, d, :DK] = i["gla_w_gk_" + s].reshape(DEPTH, RANK, GH, DK)
        gk[:, RANK, :, d, :DK] = i["gla_b_gk_" + s].reshape(DEPTH, GH, DK)
    out = {
        "x_t": np.ascontiguousarray(x.T.reshape(KD, P, NT).transpose(1, 0, 2)),
        "c_t": np.ascontiguousarray(np.stack([i["c"][0], i["c_ctx"]], 1).reshape(KD, P, 2).transpose(1, 0, 2).reshape(P, -1)),
        "vec": np.ascontiguousarray(vec.transpose(1, 0, 2).reshape(P, -1)),
        "w_mod": _tiles(i["mod_w"], np.arange(6 * D).reshape(-1, P)),
        "w_inp": _tiles(i["w_in"], _in_columns()),
        "w_outp": _tiles(np.concatenate(blocks, 1), cols),
        "w_up": _tiles(i["ffn_w_12"], up),
        "w_uq": np.ascontiguousarray(i["mla_w_uq"].reshape(DEPTH, 2, QH, -1).transpose(0, 2, 1, 3).reshape(DEPTH, QH, -1)),
        "w_ukv": np.ascontiguousarray(i["mla_w_ukv"][:, :, np.concatenate([kv[:, :NOPE].ravel(), kv[:, NOPE:].ravel()])]),
        "w_gk": np.ascontiguousarray(gk.reshape(DEPTH, RANK + 1, -1)),
    }
    r = 0
    for p, n in enumerate(PARTS):
        out[f"w_dn{p}"] = _tiles(i["ffn_w_down"][:, r * P:(r + n) * P], cols)
        r += n
    return out | _constants()


_ORDER = ["x_t", "c_t", "vec", "w_mod", "w_inp", "w_four_x", "w_four_c", "w_outp", "w_up", "w_dn0", "w_dn1", "w_dn2",
          "w_uq", "w_ukv", "w_gk", "k_ident", "k_tri", "k_mask", "k_rope", "k_rot", "k_dft"]


def kernel(**inputs):
    import concourse.bacc as bacc
    from concourse.bass_utils import run_bass_kernel_spmd

    nc = bacc.Bacc("TRN2", target_bir_lowering=False, num_devices=1)
    arrays = _layout({k: np.asarray(v) for k, v in inputs.items()})
    args = [nc.dram_tensor(f"in_{k}", arrays[k].shape, mybir.dt.from_np(arrays[k].dtype), kind="ExternalInput").ap() for k in _ORDER]
    args.append(nc.dram_tensor("out_t", (P, KD, NX), F32, kind="ExternalOutput").ap())
    build_trunk(nc, *args)
    r = run_bass_kernel_spmd(nc, [{f"in_{k}": arrays[k] for k in _ORDER}], core_ids=[0])
    o = r.results[0]["out_t"]
    return np.ascontiguousarray(o.transpose(1, 0, 2).reshape(D, NX).T)[None]
```

```python
from contextlib import ExitStack

import concourse.bass as bass
import numpy as np
from concourse import mybir

F32 = mybir.dt.float32
F32R = mybir.dt.float32r
I32 = mybir.dt.int32
ALU = mybir.AluOpType
ACT = mybir.ActivationFunctionType
AX_X = mybir.AxisListType.X

DEPTH, D, NX, NC = 2, 1024, 512, 256
NT = NX + NC
P = 128
KD = D // P
EPS = 1e-6
F_DIM, F_WIDTH = 64, 256
HEADS, Q_LORA, KV_LORA, NOPE, ROPE, VDIM = 6, 192, 128, 64, 32, 64
QK = NOPE + ROPE
QH = Q_LORA // 2
GH, DK, DV, RANK, CHUNK = 4, 48, 96, 16, 64
GRID_W, ROPE_BASE, GATE_NORM = 64, 10000.0, 16.0
D_FF = 2816
NPAIR = D_FF // P
SCALE = QK ** -0.5
NCH = NT // CHUNK
EXP_LN_SET = 6

RING = 4
SPLIT = 2
PARTS = (8, 8, 6)
KOUT = 9
SLOT = KOUT * P
MOD_A, MOD_B = 16, 32
NMOD = MOD_A + MOD_B
INP_UNITS = 16
(U_CQ0, U_CQ1, U_CKV, U_K01, U_K23, U_V0, U_V1, U_V2,
 U_F0, U_F1, U_Q01, U_Q23, U_G0, U_G1, U_G2, U_G3) = range(INP_UNITS)
NSPLIT = INP_UNITS + KD + 2 * NPAIR + KD * len(PARTS)


def four_tiles(l):
    return 8 if l < DEPTH - 1 else 4


def _stream():
    order = [("mod", 0, j) for j in range(MOD_A)]
    for l in range(DEPTH):
        whole = [("mod", 0, MOD_A + j) for j in range(MOD_B)] if l == 0 else []
        order += _mixed([("inp", l, u) for u in range(INP_UNITS)], whole, [])[0]
        order += [("four", l, j) for j in range(four_tiles(l))]
        order += [("out", l, u) for u in range(KD)]
        whole = [("mod", l + 1, j) for j in range(NMOD)] if l < DEPTH - 1 else []
        ahead = []
        for p, n in enumerate(PARTS):
            order += [("up", l, 2 * sum(PARTS[:p]) + i) for i in range(len(ahead), 2 * n)]
            ahead = [("up", l, 2 * sum(PARTS[:p + 1]) + i) for i in range(2)] if whole and p < len(PARTS) - 1 else []
            part, whole_p = [("dn", l, p * KD + u) for u in range(KD)], whole[p * 2 * KD:(p + 1) * 2 * KD]
            mixed, ahead = _mixed(part, whole_p, ahead)
            order += mixed
    return order


def _mixed(units, whole, following):
    if not whole:
        return units + following, following
    order, rest = units[:3], units[3:] + following
    for u in range(len(units)):
        order += whole[2 * u:2 * u + 2] + rest[:1]
        rest = rest[1:]
    return order, following


STREAM = _stream()
WHOLE = [t for t in STREAM if t[0] in ("mod", "four")]
PART_OF = {t: g for g, t in enumerate(STREAM)}
SPLITS = [t for t in STREAM if t[0] not in ("mod", "four")]
SPLIT_NO = {t: n for n, t in enumerate(SPLITS)}
WHOLE_NO = {t: n for n, t in enumerate(WHOLE)}
RAW_OF_SPLIT = [PART_OF[t] for t in SPLITS]


V_MODB, V_N1, V_N2, V_QL, V_KVL, V_QW, V_KW, V_GN, V_CONV = 0, 48, 56, 64, 66, 67, 68, 69, 70
NV = V_CONV + NPAIR * 8


def build_trunk(nc, x_t, c_t, vec, w_mod, w_inp, w_four_x, w_four_c, w_outp, w_up, w_dn0, w_dn1, w_dn2,
                w_uq, w_ukv, w_gk, k_ident, k_tri, k_mask, k_rope, k_rot, k_dft, out):
    w_dn = (w_dn0, w_dn1, w_dn2)
    place = [(nc.sbuf_base + 31) // 32 * 32]

    def at(name, shape, offset, dt=F32):
        return nc.alloc_sbuf_tensor_at(name, shape, dt, offset=offset)

    def keep(name, shape, dt=F32):
        n = int(np.prod(shape[1:])) * 4
        t = at(name, shape, place[0], dt)
        place[0] += (n + 31) // 32 * 32
        return t

    xt = keep("xt", [P, KD, NT])
    raw = [keep(f"raw{s}", [P, SLOT]) for s in range(RING)]
    whi = [keep(f"whi{s}", [P, SLOT], F32R) for s in range(SPLIT)]
    wlo = [keep(f"wlo{s}", [P, SLOT], F32R) for s in range(SPLIT)]
    ident = keep("ident", [P, P])
    ones = keep("ones", [P, P])
    tri = keep("tri", [P, 2, P])
    amask = keep("amask", [P, 2, P], I32)
    rope = keep("rope", [P, 2, NX])
    rot = keep("rot", [P, ROPE])
    dftf = keep("dftf", [P, 2 * P])
    eps = keep("eps", [P, 1])
    craw = keep("craw", [P, KD, 2])
    csil = keep("csil", [P, KD, 2])
    modv = keep("modv", [P, DEPTH, 6 * KD, 2])
    mscale = keep("mscale", [P, DEPTH, 2, KD, 2])
    par = keep("par", [P, DEPTH, NV])
    mx = keep("mx", [P, 6])
    blast = keep("blast", [P, NCH])
    decay = keep("decay", [P, NCH])
    uq = keep("uq", [QH, 2, HEADS * QK])
    ukv = keep("ukv", [P, HEADS * (NOPE + VDIM)])
    wgk = keep("wgk", [RANK + 1, GH * P])

    arena = place[0]

    def ar(name, shape, kib, dt=F32):
        return at(name, shape, arena + int(kib * 1024), dt)

    qp = ar("qp", [P, 2, NT], 0)
    kp = ar("kp", [P, 2, NT], 6)
    gs = ar("gs", [P, GH, NT], 12)
    vtok = ar("vtok", [P, 6, GH * DV], 24)
    lr = ar("lr", [32, NT], 33)
    ft = ar("ft", [P, 2, NT], 36)
    cq = ar("cq", [QH, 2, NT], 42)
    ckv = ar("ckv", [P, NT], 48)
    kpe = ar("kpe", [P, NT], 51)
    hhi = ar("hhi", [P, KD, NT], 54, F32R)
    hlo = ar("hlo", [P, KD, NT], 78, F32R)
    vt = ar("vt", [P, 3, NT], 102)
    rstd = ar("rstd", [P, NT], 102)
    sq = [ar(f"sq{i}", [P, NT], 105 + 3 * i) for i in range(2)]
    xn = [ar(f"xn{i}", [P, NT], 111 + 3 * i) for i in range(2)]
    ssum = ar("ssum", [P, NT], 117)
    mixfa = ar("mixfa", [P, 5, NT], 54)
    gdft = ar("gdft", [P, 6, 4 * P], 69)
    qh = [ar(f"qh{i}", [QK + 1, NT], 69 + 3 * i) for i in range(2)]
    kh = [ar(f"kh{i}", [QK + 1, NT], 75 + 3 * i) for i in range(2)]
    vall = ar("vall", [P, 6, HEADS // 2, 3 * VDIM], 81)
    pt = ar("pt", [P, 6, NT], 94.5)
    rsq = ar("rsq", [P, NT], 112.5)
    rsk = ar("rsk", [P, NT], 115.5)
    ksq = ar("ksq", [P, NT], 118.5)
    rtmp = ar("rtmp", [P, NX], 121.5)
    rsum = ar("rsum", [P, NT], 123.5)
    qsq = [ar(f"qsq{i}", [P, NT], 36 + 3 * i) for i in range(2)]
    diag = ar("diag", [P, 6, P], 39)
    gtok = ar("gtok", [P, 6, GH * P], 36)
    e_pos = ar("e_pos", [P, NT], 48)
    e_neg = ar("e_neg", [P, NT], 51)
    e_out = ar("e_out", [P, NT], 69)
    qr = ar("qr", [P, NT], 72)
    kr = ar("kr", [P, NT], 75)
    kin = ar("kin", [P, NT], 78)
    ktok = ar("ktok", [P, 6, P], 81)
    st = ar("st", [P, NCH, DV], 84)
    am = [ar(f"am{i}", [P, NT], 89 + 3 * i) for i in range(2)]
    osq = ar("osq", [P, NT], 95)
    ors = ar("ors", [P, NT], 98)
    ga = ar("ga", [P, 2 * NX], 101)
    ot = ar("ot", [P, NT], 105)
    mhi = ar("mhi", [P, KOUT, NT], 69, F32R)
    mlo = ar("mlo", [P, KOUT, NT], 24, F32R)
    fhi = ar("fhi", [P, max(PARTS), NT], 0, F32R)
    flo = ar("flo", [P, max(PARTS), NT], 24, F32R)
    ca = [ar(f"ca{i}", [P, NT], 102 + 3 * i) for i in range(2)]
    cb = [ar(f"cb{i}", [P, NT], 108 + 3 * i) for i in range(2)]
    cf = [ar(f"cf{i}", [P, NT], 114 + 3 * i) for i in range(2)]

    def width(l):
        return NT if l < DEPTH - 1 else NX

    def chunks(n):
        return [(0, NX), (NX, NT)][: 1 if n == NX else 2]

    def streams(n):
        return [(0, NX, 0), (NX, NT, 1)][: 1 if n == NX else 2]

    def s_base(l):
        return l * NSPLIT

    S_OUT = INP_UNITS

    def s_up(p):
        return INP_UNITS + KD + sum(2 * PARTS[q] + KD for q in range(p))

    def pair_base(l, p):
        return l * NPAIR + sum(PARTS[:p])

    KEY_TILES = (4, 5, 0, 1, 2, 3)
    KEY_BANK = (0, 2, 0, 2, 1, 3)

    def u_col(c):
        return (4 + 2 * (c % 2) + c // 2 // 3) * 512 + (c // 2 % 3) * DV

    with ExitStack() as ctx:
        ps = ctx.enter_context(nc.psum_tensor("ps", [P, 8 * 512], F32))

        def acc(s, a=0, b=NT, rows=(0, P)):
            return ps[rows[0]:rows[1], s * 1024 + a:s * 1024 + b]

        def bank(k, a=0, b=512, rows=(0, P)):
            return ps[rows[0]:rows[1], k * 512 + a:k * 512 + b]

        def sem(name):
            return ctx.enter_context(nc.semaphore(name))

        const_in, table_in, x_in, small_in, stored = (sem(n) for n in ("const_in", "table_in", "x_in", "small_in", "stored"))
        raw_in = [sem(f"raw_in{s}") for s in range(RING)]
        whole_used = sem("whole_used")
        hi_ready, lo_ready = sem("hi_ready"), sem("lo_ready")
        unit_done = sem("unit_done")
        pe_bar, act_bar, dve_bar = sem("pe_bar"), sem("act_bar"), sem("dve_bar")
        act_step, dve_step = sem("act_step"), sem("dve_step")
        ready0, csil_ready = sem("ready0"), sem("csil_ready")
        mod_ready = sem("mod_ready")
        sq_ready, sq_used, ssq_done = sem("sq_ready"), sem("sq_used"), sem("ssq_done")
        rstd_ready, xn_ready, ssum_ready, modn_ready = (sem(n) for n in ("rstd_ready", "xn_ready", "ssum_ready", "modn_ready"))
        hh_ready, h_ready = sem("hh_ready"), sem("h_ready")
        evac_a, evac_d = sem("evac_a"), sem("evac_d")
        vtr_done, vtr_a, vtr_d = sem("vtr_done"), sem("vtr_a"), sem("vtr_d")
        gd_done, gd_a, gd_d, four_done = sem("gd_done"), sem("gd_a"), sem("gd_d"), sem("four_done")
        lat_sq, lat_ssq, lat_rs, lat_n = sem("lat_sq"), sem("lat_ssq"), sem("lat_rs"), sem("lat_n")
        kpw_ready, kpe_rot, va_done, va_a, va_d = sem("kpw_ready"), sem("kpe_rot"), sem("va_done"), sem("va_a"), sem("va_d")
        q_raw, q_sq, q_ssq, rq_ready, qn_ready, q_rot = (sem(n) for n in ("q_raw", "q_sq", "q_ssq", "rq_ready", "qn_ready", "q_rot"))
        k_raw, k_sq, k_ssq, rk_ready, qk_ready = (sem(n) for n in ("k_raw", "k_sq", "k_ssq", "rk_ready", "qk_ready"))
        s_done, sc_done, mx_ready, diag_ready, row_done, row_ready = (sem(n) for n in ("s_done", "sc_done", "mx_ready", "diag_ready", "row_done", "row_ready"))
        st_done, p_exp, pv_done, o_out = sem("st_done"), sem("p_exp"), sem("pv_done"), sem("o_out")
        z_done, ls_ready, g_ready = sem("z_done"), sem("ls_ready"), sem("g_ready")
        b_done, e_ready, eo_raw, eo_ready, gq_ready, gk_ready = (sem(n) for n in ("b_done", "e_ready", "eo_raw", "eo_ready", "gq_ready", "gk_ready"))
        kt_done, ktok_ready, ud_done, st_ready, a_done, am_ready = (sem(n) for n in ("kt_done", "ktok_ready", "ud_done", "st_ready", "a_done", "am_ready"))
        go_done, osq_ready, ossq_done, ors_ready, lin_ready = (sem(n) for n in ("go_done", "osq_ready", "ossq_done", "ors_ready", "lin_ready"))
        mhi_ready, mlo_ready, x_upd = sem("mhi_ready"), sem("mlo_ready"), sem("x_upd")
        center_ready, gate_ready, side_ready, silu_ready = (sem(n) for n in ("center_ready", "gate_ready", "side_ready", "silu_ready"))
        fh_ready, hidh_ready, hid_ready, kpe_sq = (sem(n) for n in ("fh_ready", "hidh_ready", "hid_ready", "kpe_sq"))

        NCONST, NTABLE = 3, 5

        class Chain:

            def __init__(self, eng, own):
                self.eng, self.own, self.n, self.off = eng, own, 0, None

            def step(self, ins):
                ins.then_inc(self.own, 1)
                self.n += 1

            def wait(self, back=0):
                n = self.n - back
                self.eng.wait_ge(self.own, n if self.off is None else self.off + n)

        block = ctx.enter_context(nc.Block())

        @block.sync
        def _(sp):
            sp.dma_start(craw[:].rearrange("p a b -> p (a b)"), c_t).then_inc(const_in, 16)
            sp.dma_start(par[:].rearrange("p a b -> p (a b)"), vec).then_inc(const_in, 16)
            sp.dma_start(ident[:], k_ident).then_inc(const_in, 16)

            def source(what, l, i):
                if what == "mod":
                    return w_mod[l, i], KD * P
                if what == "inp":
                    return w_inp[l, i], KD * P
                if what == "four":
                    return (w_four_x[i], 4 * 2 * P) if i < 4 else (w_four_c[i - 4], 2 * 2 * CHUNK)
                if what == "out":
                    return w_outp[l, i], KOUT * P
                if what == "up":
                    return w_up[l, i], KD * P
                return w_dn[i // KD][l, i % KD], PARTS[i // KD] * P

            def load(g):
                if g >= RING:
                    before = STREAM[g - RING]
                    if before in WHOLE_NO:
                        sp.wait_ge(whole_used, WHOLE_NO[before] + 1)
                    else:
                        sp.wait_ge(lo_ready, SPLIT_NO[before] + 1)
                src, w = source(*STREAM[g])
                sp.dma_start(raw[g % RING][:, 0:w], src).then_inc(raw_in[g % RING], 16)

            g = 0
            while g < len(STREAM):
                what, l, i0 = STREAM[g]
                n = 0
                while g + n < len(STREAM) and STREAM[g + n] == (what, l, i0 + n) and what == "up" and g >= RING and \
                        STREAM[g + n - RING] == (what, l, i0 + n - RING):
                    n += 1
                rounds = n // RING
                if rounds < 2:
                    load(g)
                    g += 1
                    continue
                with sp.Fori(0, rounds) as it:
                    for s in range(RING):
                        sp.wait_ge(lo_ready, it * RING + (SPLIT_NO[STREAM[g + s - RING]] + 1))
                        sp.dma_start(raw[(g + s) % RING][:, 0:KD * P], w_up[l, it * RING + (i0 + s)]).then_inc(raw_in[(g + s) % RING], 16)
                g += rounds * RING
            sp.wait_ge(x_upd, DEPTH * KD * (1 + len(PARTS)))
            sp.dma_start(out, xt[:, :, 0:NX]).then_inc(stored, 16)
            sp.wait_ge(stored, 16)

        @block.gpsimd
        def _(pool):
            for k in range(KD):
                pool.dma_start(xt[:, k, :], x_t[:, k, :]).then_inc(x_in, 16)
            pool.dma_start(tri[:].rearrange("p a b -> p (a b)"), k_tri).then_inc(table_in, 16)
            pool.dma_start(amask[:].rearrange("p a b -> p (a b)"), k_mask).then_inc(table_in, 16)
            pool.dma_start(rope[NOPE:QK, :, :].rearrange("p a b -> p (a b)"), k_rope).then_inc(table_in, 16)
            pool.dma_start(rot[NOPE:QK, :], k_rot).then_inc(table_in, 16)
            pool.dma_start(dftf[:], k_dft).then_inc(table_in, 16)
            for l in range(DEPTH):
                if l:
                    pool.wait_ge(pe_bar, 4 * l)
                pool.dma_start(uq[:].rearrange("p a b -> p (a b)"), w_uq[l]).then_inc(small_in, 16)
                pool.dma_start(ukv[:], w_ukv[l]).then_inc(small_in, 16)
                pool.dma_start(wgk[:], w_gk[l]).then_inc(small_in, 16)

        @block.tensor
        def _(pe):
            mm = nc.tensor.matmul
            bar = [0]

            def barrier():
                bar[0] += 1
                nc.tensor.drain().then_inc(pe_bar, 1)
                pe.wait_ge(act_bar, bar[0])
                pe.wait_ge(dve_bar, bar[0])

            def modulation(l, j, col):
                g = PART_OF["mod", l, j]
                pe.wait_ge(raw_in[g % RING], 16 * (g // RING + 1))
                for k in range(KD):
                    last = mm(ps[:, col:col + 2], raw[g % RING][:, k * P:(k + 1) * P], csil[:, k, :], start=(k == 0), stop=(k == KD - 1))
                last.then_inc(whole_used, 1)

            def sum_squares(n_norm, n):
                pe.wait_ge(ssum_ready, n_norm + 1)
                for a, b in chunks(n):
                    last = mm(acc(0, a, b), ones[:], ssum[:, a:b], start=True, stop=True)
                last.then_inc(ssq_done, 1)

            def product(s, slot, hi, lo, rows, n, arrives=None):
                last = len(rows) - 1
                for k, r in enumerate(rows):
                    if arrives:
                        pe.wait_ge(arrives[0], arrives[1] + k + 1)
                    wh, wl = whi[slot][0:r, k * P:(k + 1) * P], wlo[slot][0:r, k * P:(k + 1) * P]
                    for w, y in ((wh, hi), (wh, lo), (wl, hi)):
                        for a, b in chunks(n):
                            ins = mm(acc(s, a, b), w, y[0:r, k, a:b], start=(k == 0 and w is wh and y is hi),
                                     stop=(k == last and w is wl))
                ins.then_inc(unit_done, 1)

            pe.wait_ge(const_in, 16 * NCONST)
            pe.wait_ge(table_in, 16 * NTABLE)
            pe.wait_ge(ready0, 1)
            pe.wait_ge(csil_ready, 1)
            for l in range(DEPTH):
                n = width(l)
                if l:
                    pe.wait_ge(x_upd, l * KD * 4)
                else:
                    for j in range(MOD_A):
                        modulation(0, j, 6 * 512 + 2 * j)
                sum_squares(2 * l, NT)

                for u in range(INP_UNITS):
                    pe.wait_ge(lo_ready, s_base(l) + u + 1)
                    if u >= 3 and u % 2:
                        pe.wait_ge(evac_a, l * 10 + (u - 3) // 2 + 1)
                    elif u >= 3:
                        pe.wait_ge(evac_d, l * 6 + (u - 4) // 2 + 1 if u < 15 else l * 6 + 6)
                    product(u % 3, u % 2, hhi, hlo, [P] * KD, NT if u < U_F0 or l < DEPTH - 1 else NX,
                            arrives=None if u else (h_ready, 2 * l * KD))
                    if l == 0:
                        for j in range(2):
                            modulation(0, MOD_A + 2 * u + j, 7 * 512 + 2 * (2 * u + j))
                if l == 0:
                    pe.wait_ge(mod_ready, 2)
                barrier()

                for tt in range(6):
                    for j in range(3):
                        last = nc.tensor.transpose(bank(tt, j * P, (j + 1) * P), vt[:, j, tt * P:(tt + 1) * P], ident[:])
                    last.then_inc(vtr_done, 1)
                for tt in range(n // P):
                    if tt >= 2:
                        pe.wait_ge(gd_a if tt % 2 else gd_d, 3 * l + tt // 2)
                    for f in range(2):
                        last = mm(bank(6 + tt % 2, f * 2 * P, (f + 1) * 2 * P), ft[:, f, tt * P:(tt + 1) * P], dftf[:], start=True, stop=True)
                    last.then_inc(gd_done, 1)
                pe.wait_ge(vtr_d, 3 * l + 3)
                pe.wait_ge(vtr_a, 3 * l + 3)
                pe.wait_ge(gd_a, 3 * l + n // (2 * P))
                pe.wait_ge(gd_d, 3 * l + n // (2 * P))
                for blk in range(four_tiles(l)):
                    g = PART_OF["four", l, blk]
                    pe.wait_ge(raw_in[g % RING], 16 * (g // RING + 1))
                    kt, w, first = (4, P, 0) if blk < 4 else (2, CHUNK, 4)
                    for f in range(2):
                        o = bank(f, blk * P, (blk + 1) * P) if blk < 4 else bank(2, f * NC + (blk - 4) * CHUNK, f * NC + (blk - 3) * CHUNK)
                        for k in range(kt):
                            for cs in range(2):
                                last = mm(o, gdft[:, first + k, f * 2 * P + cs * P:f * 2 * P + (cs + 1) * P],
                                          raw[g % RING][:, k * 2 * w + cs * w:k * 2 * w + (cs + 1) * w],
                                          start=(k == 0 and cs == 0), stop=(k == kt - 1 and cs == 1))
                    last.then_inc(whole_used, 1)
                barrier()

                pe.wait_ge(small_in, (l + 1) * 48)
                pe.wait_ge(lat_sq, 3 * l + 2)
                for a, b in chunks(NT):
                    mm(acc(0, a, b, (0, QH)), ones[0:QH, 0:QH], qsq[0][0:QH, a:b], start=True, stop=False)
                    last = mm(acc(0, a, b, (0, QH)), ones[0:QH, 0:QH], qsq[1][0:QH, a:b], start=False, stop=True)
                last.then_inc(lat_ssq, 1)
                pe.wait_ge(lat_sq, 3 * l + 3)
                for a, b in chunks(NT):
                    last = mm(acc(1, a, b), ones[:], ksq[:, a:b], start=True, stop=True)
                last.then_inc(lat_ssq, 1)
                pe.wait_ge(kpw_ready, l + 1)
                mm(acc(2, 0, NX, (NOPE, QK)), rot[NOPE:QK, :], kpe[NOPE:QK, 0:NX], start=True, stop=True).then_inc(kpe_rot, 1)
                pe.wait_ge(lat_n, 2 * l + 2)
                for tt in range(6):
                    if tt >= 2:
                        pe.wait_ge(va_a if tt % 2 else va_d, 3 * l + tt // 2)
                    mm(bank(6 + tt % 2, 0, HEADS * VDIM), ckv[:, tt * P:(tt + 1) * P],
                       ukv[:, HEADS * NOPE:HEADS * (NOPE + VDIM)], start=True, stop=True).then_inc(va_done, 1)
                pe.wait_ge(va_a, 3 * l + 3)
                pe.wait_ge(va_d, 3 * l + 3)

                def prepare(h):
                    hh = l * HEADS + h

                    def query():
                        if h:
                            pe.wait_ge(qk_ready, hh)
                        for a, b in chunks(n):
                            for k in range(2):
                                last = mm(acc(3, a, b, (0, QK)), uq[:, k, h * QK:(h + 1) * QK], cq[:, k, a:b], start=(k == 0), stop=(k == 1))
                        last.then_inc(q_raw, 1)

                    def query_squares():
                        pe.wait_ge(q_sq, hh + 1)
                        for a, b in chunks(n):
                            last = mm(acc(3, a, b, (0, QK)), ones[0:QK, 0:QK], qsq[0][0:QK, a:b], start=True, stop=True)
                        last.then_inc(q_ssq, 1)

                    def key():
                        pe.wait_ge(rq_ready, hh + 1)
                        for a, b in chunks(NT):
                            last = mm(acc(3, a, b, (0, NOPE)), ukv[:, h * NOPE:(h + 1) * NOPE], ckv[:, a:b], start=True, stop=True)
                        last.then_inc(k_raw, 1)

                    def key_squares():
                        pe.wait_ge(k_sq, hh + 1)
                        for a, b in chunks(NT):
                            last = mm(acc(3, a, b, (0, QK)), ones[0:QK, 0:QK], ksq[0:QK, a:b], start=True, stop=True)
                        last.then_inc(k_ssq, 1)

                    def partner():
                        pe.wait_ge(rk_ready, hh + 1)
                        pe.wait_ge(qn_ready, hh + 1)
                        mm(acc(3, 0, NX, (NOPE, QK)), rot[NOPE:QK, :], qh[h % 2][NOPE:QK, 0:NX], start=True, stop=True).then_inc(q_rot, 1)

                    return query, query_squares, key, key_squares, partner

                for piece in prepare(0):
                    piece()
                for h in range(HEADS):
                    hh = l * HEADS + h
                    q_, k_ = qh[h % 2], kh[h % 2]
                    following = iter(prepare(h + 1) if h + 1 < HEADS else ())

                    def next_piece():
                        piece = next(following, None)
                        if piece:
                            piece()

                    def scores(j, s):
                        for a, b in chunks(NT):
                            last = mm(acc(s, a, b), q_[0:QK, j * P:(j + 1) * P], k_[0:QK, a:b], start=True, stop=True)
                        last.then_inc(s_done, 1)

                    def shifted(i):
                        kt = KEY_TILES[i]
                        for a, b in chunks(n) if kt >= 4 else [(0, NX)]:
                            o = KEY_BANK[i] * 512
                            last = mm(ps[:, o + a:o + b], k_[:, kt * P:(kt + 1) * P], q_[:, a:b], start=True, stop=True)
                        last.then_inc(st_done, 1)

                    def values(i):
                        kt = KEY_TILES[i]
                        pe.wait_ge(p_exp, 6 * hh + i + 1)
                        v = vall[:, kt, h // 2, VDIM * (h % 2):VDIM * (h % 2) + P]
                        for a, b in chunks(n) if kt >= 4 else [(0, NX)]:
                            last = mm(acc(2, a, b), v, pt[:, kt, a:b], start=(i == 0), stop=(i == (5 if a == 0 else 1)))
                        if i == 5:
                            last.then_inc(pv_done, 1)

                    pe.wait_ge(qk_ready, hh + 1)
                    if h:
                        pe.wait_ge(p_exp, 6 * hh)
                    scores(0, 0)
                    scores(1, 1)
                    next_piece()
                    if h:
                        pe.wait_ge(o_out, hh)
                    scores(2, 2)
                    pe.wait_ge(mx_ready, 4 * hh + 1)
                    scores(3, 0)
                    if l < DEPTH - 1:
                        pe.wait_ge(mx_ready, 4 * hh + 2)
                        for j in range(2):
                            last = mm(acc(1, j * NC, (j + 1) * NC), q_[0:QK, NX + j * P:NX + (j + 1) * P], k_[0:QK, NX:NT], start=True, stop=True)
                        last.then_inc(sc_done, 1)
                    next_piece()
                    pe.wait_ge(diag_ready, hh + 1)
                    for a, b in chunks(n):
                        last = mm(acc(2, a, b), ones[:], diag[:].rearrange("p a b -> p (a b)")[:, a:b], start=True, stop=True)
                    last.then_inc(row_done, 1)
                    next_piece()
                    pe.wait_ge(row_ready, hh + 1)
                    shifted(0)
                    shifted(1)
                    next_piece()
                    pe.wait_ge(p_exp, 6 * hh + 1)
                    shifted(2)
                    values(0)
                    pe.wait_ge(p_exp, 6 * hh + 2)
                    shifted(3)
                    values(1)
                    next_piece()
                    shifted(4)
                    values(2)
                    shifted(5)
                    for i in range(3, 6):
                        values(i)
                barrier()

                for tt in range(6):
                    mm(bank(tt), lr[0:RANK + 1, tt * P:(tt + 1) * P], wgk[:], start=True, stop=True).then_inc(z_done, 1)
                pe.wait_ge(g_ready, 3 * (l + 1))
                for h in range(GH):
                    hh = l * GH + h
                    if h:
                        pe.wait_ge(lin_ready, hh)
                    for tt in range(6):
                        for d in range(2):
                            last = mm(acc(0, tt * P, (tt + 1) * P, (64 * d, 64 * d + 64)), gtok[:, tt, h * P + 64 * d:h * P + 64 * d + 64],
                                      tri[:, d, :], start=True, stop=True)
                    last.then_inc(b_done, 1)
                    pe.wait_ge(gk_ready, hh + 1)
                    for tt in range(6):
                        last = nc.tensor.transpose(acc(1, tt * P, (tt + 1) * P), kr[:, tt * P:(tt + 1) * P], ident[:])
                    last.then_inc(kt_done, 1)
                    pe.wait_ge(gq_ready, hh + 1)
                    for d in range(2):
                        if d:
                            pe.wait_ge(ktok_ready, hh + 1)
                        for tt in range(n // P):
                            t0 = tt * P
                            last = mm(acc(d, t0, t0 + P), kin[64 * d:64 * d + DK, t0:t0 + P], qr[64 * d:64 * d + DK, t0:t0 + P], start=True, stop=True)
                        last.then_inc(a_done, 1)
                    for c in range(NCH):
                        r = 64 * (c % 2)
                        last = mm(ps[:, u_col(c):u_col(c) + DV], ktok[r:r + 64, c // 2, :], vtok[r:r + 64, c // 2, h * DV:(h + 1) * DV], start=True, stop=True)
                    last.then_inc(ud_done, 1)
                    pe.wait_ge(am_ready, 2 * hh + 2)
                    pe.wait_ge(st_ready, hh + 1)
                    for tt in range(n // P):
                        o = (tt * P, (tt + 1) * P)
                        for d in range(2):
                            mm(acc(1, *o, (0, DV)), vtok[:, tt, h * DV:(h + 1) * DV],
                               am[d][:, tt * P:(tt + 1) * P], start=(d == 0), stop=False)
                        for j in range(2):
                            c = 2 * tt + j
                            last = mm(acc(1, c * CHUNK, (c + 1) * CHUNK, (0, DV)), st[:, c, :], qr[:, c * CHUNK:(c + 1) * CHUNK],
                                      start=False, stop=(j == 1))
                    last.then_inc(go_done, 1)
                    pe.wait_ge(osq_ready, hh + 1)
                    for a, b in chunks(n):
                        last = mm(acc(2, a, b, (0, DV)), ones[0:DV, 0:DV], osq[0:DV, a:b], start=True, stop=True)
                    last.then_inc(ossq_done, 1)
                barrier()

                for u in range(KD):
                    pe.wait_ge(lo_ready, s_base(l) + S_OUT + u + 1)
                    if u >= 4:
                        pe.wait_ge(x_upd, l * KD * 4 + u - 3)
                    product(u % 4, u % 2, mhi, mlo, [P] * 5 + [DV] * 4, n, arrives=None if u else (mlo_ready, l * KOUT))

                pe.wait_ge(x_upd, l * KD * 4 + KD)
                sum_squares(2 * l + 1, n)
                for p, np_ in enumerate(PARTS):
                    s0, p0 = s_base(l) + s_up(p), pair_base(l, p)
                    xu = l * KD * 4 + (1 + p) * KD

                    def up_pair(s_at, free, s, arrives=None):
                        for ab in range(2):
                            pe.wait_ge(lo_ready, s_at + (2 * s + ab + 1))
                            if ab == 0:
                                free()
                            product(2 * s + ab, ab, hhi, hlo, [P] * KD, n, None if ab else arrives)

                    for s in range(2):
                        up_pair(s0, lambda: pe.wait_ge(x_upd, xu), s, (h_ready, (2 * l + 1) * KD) if p == 0 and s == 0 else None)
                    with pe.Fori(1, np_ // 2) as it:
                        for s in range(2):
                            up_pair(it * 4 + s0, lambda: pe.wait_ge(side_ready, it * 2 + (p0 + s - 1)), s)
                    pe.wait_ge(side_ready, p0 + np_)
                    pe.wait_ge(hid_ready, p0 + np_)
                    for u in range(KD):
                        pe.wait_ge(lo_ready, s0 + 2 * np_ + u + 1)
                        if u >= 3:
                            pe.wait_ge(x_upd, xu + u - 2)
                        product(u % 3, u % 2, fhi, flo, [P] * np_, n)
                        if l < DEPTH - 1:
                            for j in range(2):
                                modulation(l + 1, (p * KD + u) * 2 + j, (6 + p % 2) * 512 + 2 * (2 * u + j))
                    if l < DEPTH - 1:
                        pe.wait_ge(modn_ready, l * len(PARTS) + p + 1)

        @block.scalar
        def _(act):
            A = nc.scalar.activation
            copy = nc.scalar.copy
            me = Chain(act, act_step)
            bar = [0]

            def barrier():
                bar[0] += 1
                nc.scalar.drain().then_inc(act_bar, 1)
                act.wait_ge(pe_bar, bar[0])
                act.wait_ge(dve_bar, bar[0])

            def exp_and_ln():
                act.add_instruction(mybir.InstLoadActFuncSet(name=nc.get_next_instruction_name(), act_func_set_id=EXP_LN_SET))

            def high(n, w):
                g = RAW_OF_SPLIT[n]
                act.wait_ge(raw_in[g % RING], 16 * (g // RING + 1))
                if n >= SPLIT:
                    act.wait_ge(unit_done, n - 1)
                copy(whi[n % SPLIT][:, 0:w], raw[g % RING][:, 0:w]).then_inc(hi_ready, 1)

            def inverse_rms(out_, in_, count, done):
                rows = out_.shape[0]
                me.step(A(out_, in_, ACT.Ln, bias=eps[0:rows, :], scale=1.0 / count))
                me.wait()
                A(out_, out_, ACT.Exp, scale=-0.5).then_inc(done, 1)

            def square(nn, k, n):
                if nn % 2:
                    act.wait_ge(x_upd, (nn // 2) * KD * 4 + k + 1)
                elif nn:
                    act.wait_ge(x_upd, (nn // 2) * KD * 4 - KD + k + 1)
                if k >= 2:
                    act.wait_ge(sq_used, nn * (KD - 2) + max(1, k - 2))
                A(sq[k % 2][:, 0:n], xt[:, k, 0:n], ACT.Square).then_inc(sq_ready, 1)

            def norm(l, which, n):
                nn = 2 * l + which
                exp_and_ln()
                act.wait_ge(ssq_done, nn + 1)
                inverse_rms(rstd[:, 0:n], acc(0, 0, n), D, rstd_ready)
                for k in range(KD):
                    act.wait_ge(xn_ready, nn * KD + k + 1)
                    for a, b, c in streams(n):
                        last = A(hhi[:, k, a:b], xn[k % 2][:, a:b], ACT.Identity, bias=modv[:, l, 3 * which * KD + k, c:c + 1])
                    last.then_inc(hh_ready, 1)

            act.wait_ge(const_in, 16 * NCONST)
            act.wait_ge(table_in, 16 * NTABLE)
            act.wait_ge(ready0, 1)
            A(csil[:], craw[:], ACT.Silu).then_inc(csil_ready, 1)
            act.wait_ge(x_in, 16 * KD)
            for k in range(KD):
                square(0, k, NT)
            for l in range(DEPTH):
                n = width(l)
                sb = s_base(l)
                if l == 0:
                    for u in range(2):
                        high(sb + u, KD * P)
                norm(l, 0, NT)

                if l:
                    for u in range(2):
                        high(sb + u, KD * P)
                for u in range(INP_UNITS):
                    if u + 2 < INP_UNITS:
                        high(sb + u + 2, KD * P)
                    if u % 2 and u < U_G0:
                        continue
                    act.wait_ge(unit_done, sb + u + 1)
                    s = u % 3
                    if u == U_CQ0:
                        copy(lr[0:RANK, :], acc(s, 0, NT, (QH, QH + RANK)))
                        ins = copy(cq[:, 0, :], acc(s, 0, NT, (0, QH)))
                    elif u == U_CKV:
                        ins = copy(ckv[:], acc(s))
                    elif u == U_K23:
                        ins = copy(kp[:, 1, :], acc(s))
                    elif u == U_V1:
                        ins = copy(vt[:, 1, :], acc(s))
                    elif u == U_F0:
                        ins = copy(ft[:, 0, 0:n], acc(s, 0, n))
                    elif u == U_Q01:
                        ins = nc.scalar.mul(qp[:, 0, 0:n], acc(s, 0, n), DK ** -0.5)
                    else:
                        ins = A(gs[0:DV, u - U_G0, 0:n], acc(s, 0, n, (0, DV)), ACT.Silu)
                    ins.then_inc(evac_a, 1)
                barrier()

                for tt in range(1, 6, 2):
                    act.wait_ge(vtr_done, 6 * l + tt + 1)
                    copy(vtok[:, tt, :], bank(tt, 0, GH * DV)).then_inc(vtr_a, 1)
                for tt in range(1, n // P, 2):
                    act.wait_ge(gd_done, 6 * l + tt + 1)
                    copy(gdft[:, tt, :], bank(6 + tt % 2)).then_inc(gd_a, 1)
                act.wait_ge(whole_used, WHOLE_NO["four", l, 3] + 1)
                copy(mixfa[:, 0, 0:NX], bank(0))
                barrier()

                exp_and_ln()
                A(qsq[0][0:QH, :], cq[:, 0, :], ACT.Square).then_inc(lat_sq, 1)
                A(qsq[1][0:QH, :], cq[:, 1, :], ACT.Square).then_inc(lat_sq, 1)
                A(ksq[:], ckv[:], ACT.Square).then_inc(lat_sq, 1)
                act.wait_ge(lat_ssq, 2 * l + 1)
                inverse_rms(rsq[0:QH, :], acc(0, 0, NT, (0, QH)), Q_LORA, lat_rs)
                act.wait_ge(lat_ssq, 2 * l + 2)
                inverse_rms(rsk[:], acc(1), KV_LORA, lat_rs)
                A(ksq[NOPE:QK, :], kpe[NOPE:QK, :], ACT.Square).then_inc(kpe_sq, 1)
                for tt in range(1, 6, 2):
                    act.wait_ge(va_done, 6 * l + tt + 1)
                    copy(vall[:, tt, :, :].rearrange("p i (b v) -> p i b v", b=3)[:, :, 0:3:2, :],
                         bank(6 + tt % 2, 0, HEADS * VDIM).rearrange("p (i b v) -> p i b v", i=HEADS // 2, b=2)).then_inc(va_a, 1)

                def prepare(h):
                    hh = l * HEADS + h

                    def query():
                        act.wait_ge(q_raw, hh + 1)
                        A(qh[h % 2][0:QK, 0:n], acc(3, 0, n, (0, QK)), ACT.Identity, scale=par[0:QK, l, V_QW:V_QW + 1])
                        A(qsq[0][0:QK, 0:n], acc(3, 0, n, (0, QK)), ACT.Square).then_inc(q_sq, 1)

                    def query_rms():
                        act.wait_ge(q_ssq, hh + 1)
                        inverse_rms(rsq[0:QK, 0:n], acc(3, 0, n, (0, QK)), QK, rq_ready)

                    def key():
                        act.wait_ge(k_raw, hh + 1)
                        A(kh[h % 2][0:NOPE, :], acc(3, 0, NT, (0, NOPE)), ACT.Identity, scale=par[0:NOPE, l, V_KW:V_KW + 1])
                        A(ksq[0:NOPE, :], acc(3, 0, NT, (0, NOPE)), ACT.Square).then_inc(k_sq, 1)

                    def key_rms():
                        act.wait_ge(k_ssq, hh + 1)
                        inverse_rms(rsk[0:QK, :], acc(3, 0, NT, (0, QK)), QK, rk_ready)

                    return query, query_rms, key, key_rms

                for piece in prepare(0):
                    piece()
                for h in range(HEADS):
                    hh = l * HEADS + h
                    following = prepare(h + 1) if h + 1 < HEADS else None

                    def exp_of(i):
                        kt = KEY_TILES[i]
                        w = n if kt >= 4 else NX
                        act.wait_ge(st_done, 6 * hh + i + 1)
                        o = KEY_BANK[i] * 512
                        A(pt[:, kt, 0:w], ps[:, o:o + w], ACT.Exp, scale=SCALE).then_inc(p_exp, 1)

                    if following:
                        for piece in following[:3]:
                            piece()
                    exp_of(0)
                    exp_of(1)
                    if following:
                        following[3]()
                    for i in range(2, 6):
                        exp_of(i)
                barrier()

                for i in range(3):
                    act.wait_ge(z_done, 6 * l + 2 * i + 2)
                    if i:
                        act.wait_ge(g_ready, 3 * l + i)
                    me.step(A(ga[:], ps[:, i * 1024:(i + 1) * 1024], ACT.Abs))
                    me.wait()
                    me.step(A(ga[:], ga[:], ACT.Exp, scale=-1.0))
                    me.wait()
                    A(ga[:], ga[:], ACT.Ln, bias=ones[:, 0:1]).then_inc(ls_ready, 1)
                for h in range(GH):
                    hh = l * GH + h
                    act.wait_ge(eo_raw, hh + 1)
                    A(e_pos[:], acc(0), ACT.Exp).then_inc(e_ready, 1)
                    A(e_neg[:], acc(0), ACT.Exp, scale=-1.0).then_inc(e_ready, 1)
                    A(decay[:], blast[:], ACT.Exp).then_inc(e_ready, 1)
                    A(e_out[:], e_out[:], ACT.Exp).then_inc(e_ready, 1)
                    act.wait_ge(kt_done, hh + 1)
                    copy(ktok[:].rearrange("p a b -> p (a b)"), acc(1)).then_inc(ktok_ready, 1)
                    act.wait_ge(go_done, hh + 1)
                    A(osq[0:DV, 0:n], acc(1, 0, n, (0, DV)), ACT.Square).then_inc(osq_ready, 1)
                    act.wait_ge(ossq_done, hh + 1)
                    inverse_rms(ors[0:DV, 0:n], acc(2, 0, n, (0, DV)), DV, ors_ready)
                barrier()

                n0 = sb + S_OUT
                high(n0, KOUT * P)
                for m in range(KOUT):
                    if m < 5:
                        copy(mhi[:, m, 0:n], mixfa[:, m, 0:n]).then_inc(mhi_ready, 1)
                    else:
                        copy(mhi[0:DV, m, 0:n], gs[0:DV, m - 5, 0:n]).then_inc(mhi_ready, 1)
                    if m == 0:
                        high(n0 + 1, KOUT * P)
                for u in range(KD):
                    high(n0 + u + 2, KOUT * P if u + 2 < KD else KD * P)
                    square(2 * l + 1, u, n)

                norm(l, 1, n)
                for p, np_ in enumerate(PARTS):
                    i0 = s_up(p) - S_OUT
                    p0 = pair_base(l, p)

                    def round_(it):
                        q_at = p0 if it is None else it * 2 + p0
                        for s in range(2):
                            for ab, c in ((0, ca), (1, cb)):
                                i = 2 * s + ab
                                g = RAW_OF_SPLIT[n0 + i0 + i + 2]
                                act.wait_ge(raw_in[g % RING], 16 * (g // RING + 1) if it is None else it * 16 + 16 * (g // RING + 1))
                                done = n0 + i0 + i + 1
                                act.wait_ge(unit_done, done if it is None else it * 4 + done)
                                copy(whi[ab][:, 0:KD * P], raw[g % RING][:, 0:KD * P]).then_inc(hi_ready, 1)
                                if ab == 0 and (it is not None or p0 > 0):
                                    act.wait_ge(fh_ready, q_at + (s - 1))
                                col = V_CONV + (sum(PARTS[:p]) + s) * 8 + 4 * ab
                                w1, b0 = [par[:, l, col + o:col + o + 1] if it is None else par[:, l, bass.ds(it * 16 + (col + o), 1)]
                                          for o in (1, 3)]
                                A(c[s][:, 0:n], acc(i, 0, n), ACT.Identity, bias=b0, scale=w1).then_inc(center_ready, 1)
                            act.wait_ge(gate_ready, q_at + (s + 1))
                            A(ca[s][:, 0:n], ca[s][:, 0:n], ACT.Silu).then_inc(silu_ready, 1)
                            act.wait_ge(fh_ready, q_at + (s + 1))
                            to = fhi[:, s:s + 1, 0:n] if it is None else fhi[:, bass.ds(it * 2 + s, 1), 0:n]
                            copy(to, cf[s][:, 0:n].rearrange("p (a b) -> p a b", a=1)).then_inc(hidh_ready, 1)

                    round_(None)
                    with act.Fori(1, np_ // 2) as it:
                        round_(it)
                    for u in range(KD):
                        i = i0 + 2 * np_ + u + 2
                        if u + 2 < KD:
                            high(n0 + i, np_ * P)
                        elif p < len(PARTS) - 1:
                            high(n0 + i, KD * P)
                        if p == len(PARTS) - 1 and l < DEPTH - 1:
                            square(2 * l + 2, u, NT)

        @block.vector
        def _(dve):
            stt, tt_, ts = nc.vector.scalar_tensor_tensor, nc.vector.tensor_tensor, nc.vector.tensor_scalar
            copy = nc.vector.tensor_copy
            me = Chain(dve, dve_step)
            bar = [0]

            def barrier():
                bar[0] += 1
                nc.vector.drain().then_inc(dve_bar, 1)
                dve.wait_ge(pe_bar, bar[0])
                dve.wait_ge(act_bar, bar[0])

            def low(n, w):
                g = RAW_OF_SPLIT[n]
                dve.wait_ge(hi_ready, n + 1)
                tt_(wlo[n % SPLIT][:, 0:w], raw[g % RING][:, 0:w], whi[n % SPLIT][:, 0:w].bitcast(F32), ALU.subtract).then_inc(lo_ready, 1)

            def add_square(nn, k, n):
                if k == 0:
                    return
                dve.wait_ge(sq_ready, nn * KD + k + 1)
                if k > 1:
                    dve.wait_ge(sq_used, nn * (KD - 2) + k - 1)
                ins = tt_(ssum[:, 0:n], (sq[0] if k == 1 else ssum)[:, 0:n], sq[k % 2][:, 0:n], ALU.add)
                ins.then_inc(sq_used if k < KD - 1 else ssum_ready, 1)

            def norm(l, which, n):
                nn = 2 * l + which
                dve.wait_ge(rstd_ready, nn + 1)

                def low_h(k):
                    dve.wait_ge(hh_ready, nn * KD + k + 1)
                    for a, b, c in streams(n):
                        last = stt(hlo[:, k, a:b], xn[k % 2][:, a:b], modv[:, l, 3 * which * KD + k, c:c + 1],
                                   hhi[:, k, a:b].bitcast(F32), ALU.add, ALU.subtract)
                    last.then_inc(h_ready, 1)

                for k in range(KD):
                    if k > 1:
                        dve.wait_ge(h_ready, nn * KD + k - 1)
                    for a, b, c in streams(n):
                        last = stt(xn[k % 2][:, a:b], xt[:, k, a:b], mscale[:, l, which, k, c:c + 1], rstd[:, a:b], ALU.mult, ALU.mult)
                    last.then_inc(xn_ready, 1)
                    if k:
                        low_h(k - 1)
                low_h(KD - 1)

            def modulation(l, first, cnt, src):
                bias = par[:, l, V_MODB + first:V_MODB + first + cnt].unsqueeze(2).to_broadcast([P, cnt, 2])
                return tt_(modv[:, l, first:first + cnt, :], src[:, 0:2 * cnt].rearrange("p (a b) -> p a b", b=2), bias, ALU.add)

            def norm_scale(l, which):
                sc = modv[:, l, (3 * which + 1) * KD:(3 * which + 2) * KD, :]
                v = V_N2 if which else V_N1
                nw = par[:, l, v:v + KD].unsqueeze(2).to_broadcast([P, KD, 2])
                return stt(mscale[:, l, which, :, :], sc, 1.0, nw, ALU.add, ALU.mult)

            def update(l, k, s, gate, v, n):
                if v >= KD:
                    dve.wait_ge(x_upd, v - KD + 1)
                for a, b, c in streams(n):
                    last = stt(xt[:, k, a:b], acc(s, a, b), modv[:, l, gate * KD + k, c:c + 1], xt[:, k, a:b], ALU.mult, ALU.add)
                last.then_inc(x_upd, 1)

            nc.vector.memset(ones[:], 1.0)
            nc.vector.memset(eps[:], EPS).then_inc(ready0, 1)
            dve.wait_ge(const_in, 16 * NCONST)
            dve.wait_ge(table_in, 16 * NTABLE)
            dve.wait_ge(x_in, 16 * KD)
            for k in range(KD):
                add_square(0, k, NT)
            dve.wait_ge(whole_used, MOD_A)
            me.step(modulation(0, 0, MOD_A, bank(6)))
            me.wait()
            norm_scale(0, 0).then_inc(mod_ready, 1)
            for l in range(DEPTH):
                n = width(l)
                sb = s_base(l)
                nc.vector.memset(lr[:], 1.0)
                if l:
                    dve.wait_ge(x_upd, l * KD * 4)
                else:
                    for u in range(2):
                        low(sb + u, KD * P)
                    dve.wait_ge(mod_ready, 1)
                norm(l, 0, NT)

                if l:
                    for u in range(2):
                        low(sb + u, KD * P)
                for u in range(INP_UNITS):
                    if u + 2 < INP_UNITS:
                        low(sb + u + 2, KD * P)
                    if u % 2 == 0 or u >= U_G0:
                        continue
                    dve.wait_ge(unit_done, sb + u + 1)
                    s = u % 3
                    if u == U_CQ1:
                        copy(kpe[NOPE:QK, :], acc(s, 0, NT, (QH, P)))
                        ins = copy(cq[:, 1, :], acc(s, 0, NT, (0, QH)))
                    elif u == U_K01:
                        ins = copy(kp[:, 0, :], acc(s))
                    elif u in (U_V0, U_V2):
                        ins = copy(vt[:, u - U_V0, :], acc(s))
                    elif u == U_F1:
                        ins = copy(ft[:, 1, 0:n], acc(s, 0, n))
                    else:
                        ins = ts(qp[:, 1, 0:n], acc(s, 0, n), DK ** -0.5, None, ALU.mult)
                    ins.then_inc(evac_d, 1)
                if l == 0:
                    dve.wait_ge(whole_used, NMOD)
                    me.step(modulation(0, MOD_A, MOD_B, bank(7)))
                    me.wait()
                    norm_scale(0, 1).then_inc(mod_ready, 1)
                barrier()

                for tt in range(0, 6, 2):
                    dve.wait_ge(vtr_done, 6 * l + tt + 1)
                    copy(vtok[:, tt, :], bank(tt, 0, GH * DV)).then_inc(vtr_d, 1)
                for tt in range(0, n // P, 2):
                    dve.wait_ge(gd_done, 6 * l + tt + 1)
                    copy(gdft[:, tt, :], bank(6 + tt % 2)).then_inc(gd_d, 1)
                dve.wait_ge(whole_used, WHOLE_NO["four", l, 3] + 1)
                copy(mixfa[:, 1, 0:NX], bank(1))
                if l < DEPTH - 1:
                    dve.wait_ge(whole_used, WHOLE_NO["four", l, 7] + 1)
                    copy(mixfa[:, 0:2, NX:NT], bank(2).rearrange("p (f t) -> p f t", f=2))
                barrier()

                nc.vector.memset(vall[:, :, :, VDIM:2 * VDIM].rearrange("p a i v -> p (a i) v"), 1.0)
                for i in range(2):
                    nc.vector.memset(kh[i][QK:QK + 1, :], 1.0)
                dve.wait_ge(lat_rs, 2 * l + 1)
                for j in range(2):
                    last = stt(cq[:, j, :], cq[:, j, :], par[0:QH, l, V_QL + j:V_QL + j + 1], rsq[0:QH, :], ALU.mult, ALU.mult)
                last.then_inc(lat_n, 1)
                dve.wait_ge(lat_rs, 2 * l + 2)
                stt(ckv[:], ckv[:], par[:, l, V_KVL:V_KVL + 1], rsk[:], ALU.mult, ALU.mult).then_inc(lat_n, 1)
                dve.wait_ge(kpe_sq, l + 1)
                kw = par[:, l, V_KW:V_KW + 1]
                ts(kpe[NOPE:QK, :], kpe[NOPE:QK, :], kw[NOPE:QK, :], None, ALU.mult).then_inc(kpw_ready, 1)
                dve.wait_ge(kpe_rot, l + 1)
                kx = kpe[NOPE:QK, 0:NX]
                me.step(tt_(rtmp[NOPE:QK, :], acc(2, 0, NX, (NOPE, QK)), rope[NOPE:QK, 1, :], ALU.mult))
                me.step(tt_(kx, kx, rope[NOPE:QK, 0, :], ALU.mult))
                me.wait()
                me.step(tt_(kx, kx, rtmp[NOPE:QK, :], ALU.add))
                for tt in range(0, 6, 2):
                    dve.wait_ge(va_done, 6 * l + tt + 1)
                    copy(vall[:, tt, :, :].rearrange("p i (b v) -> p i b v", b=3)[:, :, 0:3:2, :],
                         bank(6 + tt % 2, 0, HEADS * VDIM).rearrange("p (i b v) -> p i b v", i=HEADS // 2, b=2)).then_inc(va_d, 1)
                me.wait()
                def prepare(h):
                    hh = l * HEADS + h
                    q_, k_ = qh[h % 2], kh[h % 2]
                    dve.wait_ge(rq_ready, hh + 1)
                    tt_(q_[0:QK, 0:n], q_[0:QK, 0:n], rsq[0:QK, 0:n], ALU.mult).then_inc(qn_ready, 1)
                    dve.wait_ge(rk_ready, hh + 1)
                    tt_(k_[0:NOPE, :], k_[0:NOPE, :], rsk[0:NOPE, :], ALU.mult)
                    tt_(k_[NOPE:QK, :], kpe[NOPE:QK, :], rsk[NOPE:QK, :], ALU.mult)
                    dve.wait_ge(q_rot, hh + 1)
                    qx = q_[NOPE:QK, 0:NX]
                    me.step(tt_(rtmp[NOPE:QK, :], acc(3, 0, NX, (NOPE, QK)), rope[NOPE:QK, 1, :], ALU.mult))
                    me.step(tt_(qx, qx, rope[NOPE:QK, 0, :], ALU.mult))
                    me.wait()
                    tt_(qx, qx, rtmp[NOPE:QK, :], ALU.add).then_inc(qk_ready, 1)

                prepare(0)
                for h in range(HEADS):
                    hh = l * HEADS + h
                    q_ = qh[h % 2]
                    for j in range(4):
                        dve.wait_ge(s_done, 4 * hh + j + 1)
                        nc.vector.reduce_max(mx[:, j:j + 1], acc(j % 3), AX_X).then_inc(mx_ready, 1)
                    if l < DEPTH - 1:
                        dve.wait_ge(sc_done, hh + 1)
                        me.step(nc.vector.reduce_max(mx[:, 4:6], acc(1, 0, 2 * NC).rearrange("p (t k) -> p t k", t=2), AX_X))
                        me.wait()
                    dve.wait_ge(mx_ready, 4 * hh + 4)
                    nt = n // P
                    stt(diag[:, 0:nt, :], mx[:, 0:nt].unsqueeze(2).to_broadcast([P, nt, P]), -1.0,
                        ident[:].unsqueeze(1).to_broadcast([P, nt, P]), ALU.mult, ALU.mult).then_inc(diag_ready, 1)
                    dve.wait_ge(row_done, hh + 1)
                    copy(q_[QK:QK + 1, 0:n], acc(2, 0, n, (QK, QK + 1))).then_inc(row_ready, 1)
                    if h + 1 < HEADS:
                        prepare(h + 1)
                    dve.wait_ge(pv_done, hh + 1)
                    r0, r1 = VDIM * (h % 2), VDIM * (1 - h % 2)
                    me.step(nc.vector.reciprocal(rsum[r0:r0 + VDIM, 0:n], acc(2, 0, n, (r1, r1 + VDIM))))
                    me.wait()
                    tt_(mixfa[r0:r0 + VDIM, 2 + h // 2, 0:n], acc(2, 0, n, (r0, r0 + VDIM)), rsum[r0:r0 + VDIM, 0:n], ALU.mult).then_inc(o_out, 1)
                barrier()

                for t in (qr, kr, am[0], am[1]):
                    me.step(nc.vector.memset(t[:], 0.0))
                me.step(nc.vector.memset(st[:].rearrange("p a b -> p (a b)"), 0.0))
                for i in range(3):
                    dve.wait_ge(ls_ready, 3 * l + i + 1)
                    stt(gtok[:, 2 * i:2 * i + 2, :].rearrange("p a b -> p (a b)"), ps[:, i * 1024:(i + 1) * 1024], 0.0, ga[:],
                        ALU.min, ALU.subtract).then_inc(g_ready, 1)
                me.wait()
                fwd = [8, 9, 10, 11, 0, 1, 2, 3, 4, 5, 6, 7]
                bwd = [11, 10, 9, 8, 7, 6, 5, 4, 3, 2, 1, 0]
                for h in range(GH):
                    hh = l * GH + h
                    src = 64 * (h % 2)
                    for d in range(2):
                        me.step(copy(qr[64 * d:64 * d + DK, 0:n], qp[src:src + DK, h // 2, 0:n]))
                        me.step(copy(kr[64 * d:64 * d + DK, :], kp[src:src + DK, h // 2, :]))
                    dve.wait_ge(b_done, hh + 1)
                    for d, t in ((0, CHUNK - 1), (1, 0)):
                        rows = (64 * d, 64 * d + 64)
                        me.step(copy(blast[rows[0]:rows[1], :], acc(0, 0, NT, rows).rearrange("p (c t) -> p c t", t=CHUNK)[:, :, t]))
                    me.wait()
                    tt_(e_out[:].rearrange("p (c t) -> p c t", t=CHUNK), blast[:].unsqueeze(2).to_broadcast([P, NCH, CHUNK]),
                        acc(0).rearrange("p (c t) -> p c t", t=CHUNK), ALU.subtract).then_inc(eo_raw, 1)
                    dve.wait_ge(e_ready, 4 * hh + 2)
                    me.step(tt_(kin[:], kr[:], e_neg[:], ALU.mult))
                    tt_(qr[:, 0:n], qr[:, 0:n], e_pos[:, 0:n], ALU.mult).then_inc(gq_ready, 1)
                    dve.wait_ge(e_ready, 4 * hh + 4)
                    tt_(kr[:], kr[:], e_out[:], ALU.mult).then_inc(gk_ready, 1)
                    for d in range(2):
                        dve.wait_ge(a_done, 2 * hh + d + 1)
                        for t in range(n // P):
                            last = nc.vector.copy_predicated(am[d][:, t * P:(t + 1) * P], amask[:, d, :], acc(d, t * P, (t + 1) * P))
                        last.then_inc(am_ready, 1)
                    dve.wait_ge(ud_done, hh + 1)
                    for i in range(NCH - 1):
                        for d, order in ((0, fwd), (1, bwd)):
                            a, b = order[i], order[i + 1]
                            r = slice(64 * d, 64 * d + 64)
                            u = ps[r, u_col(a):u_col(a) + DV]
                            if i:
                                me.wait(1)
                            ins = stt(st[r, b, :], st[r, a, :], decay[r, a:a + 1], u, ALU.mult, ALU.add)
                            if i == NCH - 2 and d == 1:
                                ins.then_inc(st_ready, 1)
                            else:
                                me.step(ins)
                    dve.wait_ge(ors_ready, hh + 1)
                    me.step(stt(ot[0:DV, 0:n], acc(1, 0, n, (0, DV)), par[0:DV, l, V_GN:V_GN + 1], ors[0:DV, 0:n], ALU.mult, ALU.mult))
                    me.wait()
                    tt_(gs[0:DV, h, 0:n], gs[0:DV, h, 0:n], ot[0:DV, 0:n], ALU.mult).then_inc(lin_ready, 1)
                barrier()

                n0 = sb + S_OUT
                low(n0, KOUT * P)
                for m in range(KOUT):
                    dve.wait_ge(mhi_ready, l * KOUT + m + 1)
                    rows, src = (P, mixfa[:, m, 0:n]) if m < 5 else (DV, gs[0:DV, m - 5, 0:n])
                    tt_(mlo[0:rows, m, 0:n], src, mhi[0:rows, m, 0:n].bitcast(F32), ALU.subtract).then_inc(mlo_ready, 1)
                    if m == 0:
                        low(n0 + 1, KOUT * P)
                for u in range(KD):
                    low(n0 + u + 2, KOUT * P if u + 2 < KD else KD * P)
                    dve.wait_ge(unit_done, n0 + u + 1)
                    update(l, u, u % 4, 2, l * KD * 4 + u, n)
                    if u:
                        add_square(2 * l + 1, u - 1, n)
                add_square(2 * l + 1, KD - 1, n)

                norm(l, 1, n)
                for p, np_ in enumerate(PARTS):
                    i0 = s_up(p) - S_OUT
                    p0 = pair_base(l, p)

                    def round_(it):
                        q_at = p0 if it is None else it * 2 + p0
                        for s in range(2):
                            for ab, c in ((0, ca), (1, cb)):
                                i = 2 * s + ab
                                g = RAW_OF_SPLIT[n0 + i0 + i + 2]
                                hi = n0 + i0 + i + 3
                                dve.wait_ge(hi_ready, hi if it is None else it * 4 + hi)
                                tt_(wlo[ab][:, 0:KD * P], raw[g % RING][:, 0:KD * P], whi[ab][:, 0:KD * P].bitcast(F32), ALU.subtract).then_inc(lo_ready, 1)
                                dve.wait_ge(center_ready, 2 * q_at + (2 * s + ab + 1))
                                col = V_CONV + (sum(PARTS[:p]) + s) * 8 + 4 * ab
                                w0, w2 = [par[:, l, col + o:col + o + 1] if it is None else par[:, l, bass.ds(it * 16 + (col + o), 1)]
                                          for o in (0, 2)]
                                parts = streams(n)
                                for a, b, _ in parts:
                                    me.step(stt(c[s][:, a + 1:b], acc(i, a, b - 1), w0, c[s][:, a + 1:b], ALU.mult, ALU.add))
                                for a, b, _ in parts:
                                    me.wait(len(parts) - 1)
                                    ins = stt(c[s][:, a:b - 1], acc(i, a + 1, b), w2, c[s][:, a:b - 1], ALU.mult, ALU.add)
                                    if b == parts[-1][1]:
                                        ins.then_inc(side_ready if ab else gate_ready, 1)
                                    else:
                                        me.step(ins)
                            dve.wait_ge(silu_ready, q_at + (s + 1))
                            dve.wait_ge(side_ready, q_at + (s + 1))
                            tt_(cf[s][:, 0:n], ca[s][:, 0:n], cb[s][:, 0:n], ALU.mult).then_inc(fh_ready, 1)
                            dve.wait_ge(hidh_ready, q_at + (s + 1))
                            h_, l_ = [t[:, s:s + 1, 0:n] if it is None else t[:, bass.ds(it * 2 + s, 1), 0:n] for t in (fhi, flo)]
                            tt_(l_, cf[s][:, 0:n].rearrange("p (a b) -> p a b", a=1), h_.bitcast(F32), ALU.subtract).then_inc(hid_ready, 1)

                    before = me.n
                    round_(None)
                    each = me.n - before
                    before = me.n
                    with dve.Fori(1, np_ // 2) as it:
                        me.off = it * each - each
                        round_(it)
                        me.off = None
                    me.n = before + each * (np_ // 2 - 1)
                    for u in range(KD):
                        i = i0 + 2 * np_ + u + 2
                        if u + 2 < KD:
                            low(n0 + i, np_ * P)
                        elif p < len(PARTS) - 1:
                            low(n0 + i, KD * P)
                        dve.wait_ge(unit_done, n0 + i0 + 2 * np_ + u + 1)
                        update(l, u, u % 3, 5, l * KD * 4 + (1 + p) * KD + u, n)
                        if u and p == len(PARTS) - 1 and l < DEPTH - 1:
                            add_square(2 * l + 2, u - 1, NT)
                    if l < DEPTH - 1:
                        if p == len(PARTS) - 1:
                            add_square(2 * l + 2, KD - 1, NT)
                        dve.wait_ge(whole_used, WHOLE_NO["mod", l + 1, 0] + (p + 1) * 2 * KD)
                        modulation(l + 1, p * 2 * KD, 2 * KD, bank(6 + p % 2)).then_inc(modn_ready, 1)
                        dve.wait_ge(modn_ready, l * len(PARTS) + p + 1)
                        if p == len(PARTS) - 1:
                            for which in range(2):
                                last = norm_scale(l + 1, which)
                            last.then_inc(mod_ready, 1)
                            dve.wait_ge(mod_ready, l + 3)


def _tiles(w, cols):
    cols = np.asarray(cols)
    rows = w.shape[1]
    padded = np.concatenate([w, np.zeros(w.shape[:2] + (1,), w.dtype)], axis=2)[:, :, cols.reshape(-1)]
    t = padded.reshape(DEPTH, rows // P, P, cols.shape[0], P)
    return np.ascontiguousarray(t.transpose(0, 3, 2, 1, 4).reshape(DEPTH, cols.shape[0], P, rows))


def _in_columns():
    m0, g0 = F_WIDTH, F_WIDTH + Q_LORA + KV_LORA + ROPE
    q0, k0, v0 = g0, g0 + GH * DK, g0 + 2 * GH * DK
    r0, o0 = v0 + GH * DV, v0 + GH * DV + RANK

    def span(a, n, pad=0):
        return list(range(a, a + n)) + [-1] * pad

    u = [span(m0, QH) + span(r0, RANK, 16),
         span(m0 + QH, QH) + span(m0 + Q_LORA + KV_LORA, ROPE),
         span(m0 + Q_LORA, KV_LORA)]
    u += [span(k0 + 2 * i * DK, DK, 16) + span(k0 + (2 * i + 1) * DK, DK, 16) for i in range(2)]
    u += [span(v0 + i * P, P) for i in range(3)]
    u += [span(i * P, P) for i in range(2)]
    u += [span(q0 + 2 * i * DK, DK, 16) + span(q0 + (2 * i + 1) * DK, DK, 16) for i in range(2)]
    u += [span(o0 + h * DV, DV, P - DV) for h in range(GH)]
    return u


def _dft(n, block):
    t = np.arange(n)
    ang = 2 * np.pi * (np.outer(t, t) % n) / n
    norm = 1 / np.sqrt(n * F_DIM)
    cs = np.stack([np.cos(ang), -np.sin(ang)], 1) * norm
    cs = cs.reshape(n // P, P, 2, n // block, block).transpose(3, 1, 0, 2, 4)
    return np.ascontiguousarray(cs.reshape(n // block, P, -1)).astype(np.float32)


def _constants():
    s, t = np.arange(P)[:, None], np.arange(P)[None, :]
    same = s // CHUNK == t // CHUNK
    order = [same & (s <= t), same & (s >= t)]
    tri = np.stack(order, 1).astype(np.float32) / GATE_NORM
    mask = np.concatenate(order, 1).astype(np.int32)
    half = ROPE // 2
    inv = ROPE_BASE ** (-np.arange(0, half, 2) / half)
    pos = np.arange(NX)
    ang = [np.outer(inv, pos // GRID_W), np.outer(inv, pos % GRID_W)]
    ang = np.concatenate([ang[0], ang[0], ang[1], ang[1]])
    rot = np.zeros((ROPE, ROPE), np.float32)
    for b in (0, half):
        for i in range(half // 2):
            rot[b + half // 2 + i, b + i] = -1
            rot[b + i, b + half // 2 + i] = 1
    f = np.arange(F_DIM)
    a = 2 * np.pi * np.outer(f, f) / F_DIM
    dft = np.concatenate([np.kron(np.eye(2), np.cos(a)), np.kron(np.eye(2), np.sin(a))], 1)
    return {
        "k_ident": np.eye(P, dtype=np.float32), "k_tri": tri.reshape(P, -1), "k_mask": mask,
        "k_rope": np.concatenate([np.cos(ang), np.sin(ang)], 1).astype(np.float32), "k_rot": rot,
        "k_dft": dft.astype(np.float32), "w_four_x": _dft(NX, P), "w_four_c": _dft(NC, CHUNK),
    }


def _rows(v, rows=P):
    t = v.reshape(DEPTH, -1, rows).transpose(0, 2, 1)
    return np.concatenate([t, np.zeros((DEPTH, P - rows, t.shape[2]), v.dtype)], 1)


def _layout(i):
    x = np.concatenate([i["x"][0], i["ctx"][0]], 0)
    conv = np.concatenate([i["ffn_conv_w"], i["ffn_conv_b"][:, None]], 1)
    conv = conv.reshape(DEPTH, 4, 2, NPAIR, P).transpose(0, 4, 3, 2, 1).reshape(DEPTH, P, NPAIR * 8)
    vec = np.concatenate([
        _rows(i["mod_b"]), _rows(i["norm1_w"]), _rows(i["norm2_w"]), _rows(i["mla_q_lora_norm_w"], QH),
        _rows(i["mla_kv_lora_norm_w"]), _rows(i["mla_q_norm_w"], QK), _rows(i["mla_k_norm_w"], QK),
        _rows(i["gla_norm_w"], DV), conv], 2)
    wo = i["w_out"]
    blocks = [wo[:, k * P:(k + 1) * P] for k in range(5)]
    blocks += [np.concatenate([wo[:, 5 * P + h * DV:5 * P + (h + 1) * DV], np.zeros((DEPTH, P - DV, D), wo.dtype)], 1) for h in range(GH)]
    up = np.arange(2 * D_FF).reshape(2, NPAIR, P).transpose(1, 0, 2).reshape(2 * NPAIR, P)
    cols = np.arange(D).reshape(KD, P)
    kv = np.arange(HEADS * (NOPE + VDIM)).reshape(HEADS, -1)
    gk = np.zeros((DEPTH, RANK + 1, GH, 2, 64), np.float32)
    for d, s in enumerate(("fwd", "bwd")):
        gk[:, :RANK, :, d, :DK] = i["gla_w_gk_" + s].reshape(DEPTH, RANK, GH, DK)
        gk[:, RANK, :, d, :DK] = i["gla_b_gk_" + s].reshape(DEPTH, GH, DK)
    out = {
        "x_t": np.ascontiguousarray(x.T.reshape(KD, P, NT).transpose(1, 0, 2)),
        "c_t": np.ascontiguousarray(np.stack([i["c"][0], i["c_ctx"]], 1).reshape(KD, P, 2).transpose(1, 0, 2).reshape(P, -1)),
        "vec": np.ascontiguousarray(vec.transpose(1, 0, 2).reshape(P, -1)),
        "w_mod": _tiles(i["mod_w"], np.arange(6 * D).reshape(-1, P)),
        "w_inp": _tiles(i["w_in"], _in_columns()),
        "w_outp": _tiles(np.concatenate(blocks, 1), cols),
        "w_up": _tiles(i["ffn_w_12"], up),
        "w_uq": np.ascontiguousarray(i["mla_w_uq"].reshape(DEPTH, 2, QH, -1).transpose(0, 2, 1, 3).reshape(DEPTH, QH, -1)),
        "w_ukv": np.ascontiguousarray(i["mla_w_ukv"][:, :, np.concatenate([kv[:, :NOPE].ravel(), kv[:, NOPE:].ravel()])]),
        "w_gk": np.ascontiguousarray(gk.reshape(DEPTH, RANK + 1, -1)),
    }
    r = 0
    for p, n in enumerate(PARTS):
        out[f"w_dn{p}"] = _tiles(i["ffn_w_down"][:, r * P:(r + n) * P], cols)
        r += n
    return out | _constants()


_ORDER = ["x_t", "c_t", "vec", "w_mod", "w_inp", "w_four_x", "w_four_c", "w_outp", "w_up", "w_dn0", "w_dn1", "w_dn2",
          "w_uq", "w_ukv", "w_gk", "k_ident", "k_tri", "k_mask", "k_rope", "k_rot", "k_dft"]


def kernel(**inputs):
    import concourse.bacc as bacc
    from concourse.bass_utils import run_bass_kernel_spmd

    nc = bacc.Bacc("TRN2", target_bir_lowering=False, num_devices=1)
    arrays = _layout({k: np.asarray(v) for k, v in inputs.items()})
    args = [nc.dram_tensor(f"in_{k}", arrays[k].shape, mybir.dt.from_np(arrays[k].dtype), kind="ExternalInput").ap() for k in _ORDER]
    args.append(nc.dram_tensor("out_t", (P, KD, NX), F32, kind="ExternalOutput").ap())
    build_trunk(nc, *args)
    r = run_bass_kernel_spmd(nc, [{f"in_{k}": arrays[k] for k in _ORDER}], core_ids=[0])
    o = r.results[0]["out_t"]
    return np.ascontiguousarray(o.transpose(1, 0, 2).reshape(D, NX).T)[None]
```
